# Optimizing a Trainium2 kernel written in Bass

```python
import math
import jax, jax.numpy as jnp
from jax import lax
import numpy as np

D_MODEL = 1024
BATCH = 1
SEQ = 512
DEPTH = 1

CHUNK = 64
D_CONV = 1024
CONV_WIDTH = 3
HEAD_DIM = 64
N_HEADS = 16
D_ATT = N_HEADS * HEAD_DIM
Q_BLOCK = 128
N_GROUPS = 4
EXPERTS_PER_GROUP = 8
N_EXPERTS = N_GROUPS * EXPERTS_PER_GROUP
TOP_K = 2
D_EXPERT = 512
MOE_BLOCK = 256
EPS = 1e-6

SPLITS = (D_CONV, D_CONV, D_CONV, D_ATT, D_ATT, D_ATT, N_HEADS, D_MODEL, D_MODEL)
D_IN_PROJ = sum(SPLITS)


def rmsnorm(x, g):
    xf = x.astype(jnp.float32)
    y = xf * lax.rsqrt(jnp.mean(xf * xf, axis=-1, keepdims=True) + EPS)
    return (y * g.astype(jnp.float32)).astype(x.dtype)

def split_cols(p):
    idx = np.cumsum(np.array(SPLITS))[:-1].tolist()
    return jnp.split(p, idx, axis=-1)

def short_conv(b, c, u, conv_w, conv_b):
    S = u.shape[1]
    z = c * u
    zp = jnp.pad(z, ((0, 0), (CONV_WIDTH - 1, 0), (0, 0)))
    acc = conv_b
    for i in range(CONV_WIDTH):
        acc = acc + conv_w[i] * zp[:, i:i + S]
    return b * acc

def forgetting_attention(q, k, v, f_logit, b_forget):
    B, S, H, dh = q.shape
    log_f = jax.nn.log_sigmoid(f_logit.astype(jnp.float32) + b_forget.astype(jnp.float32))
    cum = jnp.transpose(jnp.cumsum(log_f, axis=1), (0, 2, 1))
    scale = 1.0 / math.sqrt(dh)
    outs = []
    for qb in range(S // Q_BLOCK):
        qs, qe = qb * Q_BLOCK, (qb + 1) * Q_BLOCK
        qblk = q[:, qs:qe]
        kp, vp = k[:, :qe], v[:, :qe]
        s = jnp.einsum('bqhd,bkhd->bhqk', qblk, kp).astype(jnp.float32) * scale
        s = s + (cum[:, :, qs:qe, None] - cum[:, :, None, :qe])
        t_pos = jnp.arange(qs, qe)[:, None]
        s_pos = jnp.arange(qe)[None, :]
        s = jnp.where(s_pos <= t_pos, s, -jnp.inf)
        p = jax.nn.softmax(s, axis=-1).astype(v.dtype)
        outs.append(jnp.einsum('bhqk,bkhd->bqhd', p, vp))
    return jnp.concatenate(outs, axis=1)

def token_mixer(h, w_in, conv_w, conv_b, b_forget, w_conv_out, w_att_out, w_out):
    B, S, _ = h.shape
    proj = h @ w_in
    cb, cc, cu, q, k, v, f_logit, g_conv, g_att = split_cols(proj)
    y_conv = short_conv(cb, cc, cu, conv_w, conv_b) @ w_conv_out
    o = forgetting_attention(q.reshape(B, S, N_HEADS, HEAD_DIM),
                             k.reshape(B, S, N_HEADS, HEAD_DIM),
                             v.reshape(B, S, N_HEADS, HEAD_DIM),
                             f_logit, b_forget)
    y_att = o.reshape(B, S, D_ATT) @ w_att_out
    m = jax.nn.sigmoid(g_conv) * y_conv + jax.nn.sigmoid(g_att) * y_att
    return m @ w_out

def hier_moe(h, w_router_group, w_router_expert, w_e_gate, w_e_up, w_e_down):
    B, S, D = h.shape
    T = B * S
    hf = h.reshape(T, D)
    pg = jax.nn.softmax((hf @ w_router_group).astype(jnp.float32), axis=-1)
    g_val, g_idx = lax.top_k(pg, 1)
    le = jnp.einsum('td,gde->tge', hf, w_router_expert).astype(jnp.float32)
    le_sel = jnp.take_along_axis(le, g_idx[:, :, None], axis=1)[:, 0]
    pe = jax.nn.softmax(le_sel, axis=-1)
    e_val, e_idx = lax.top_k(pe, TOP_K)
    e_val = e_val / jnp.sum(e_val, axis=-1, keepdims=True)
    w_tok = (g_val * e_val).astype(h.dtype)
    expert = (g_idx * EXPERTS_PER_GROUP + e_idx).astype(jnp.int32)

    A = T * TOP_K
    flat_e = expert.reshape(A)
    flat_w = w_tok.reshape(A)
    flat_tok = jnp.arange(A, dtype=jnp.int32) // TOP_K
    order = jnp.argsort(flat_e)
    sorted_e = flat_e[order]
    counts = jnp.bincount(flat_e, length=N_EXPERTS)
    padded = (counts + MOE_BLOCK - 1) // MOE_BLOCK * MOE_BLOCK
    start_sorted = jnp.cumsum(counts) - counts
    end_padded = jnp.cumsum(padded)
    start_padded = end_padded - padded
    rank = jnp.arange(A, dtype=jnp.int32) - start_sorted[sorted_e]
    dest = start_padded[sorted_e] + rank
    n_rows = A + N_EXPERTS * MOE_BLOCK
    n_blocks = n_rows // MOE_BLOCK
    row_tok = jnp.zeros((n_rows,), jnp.int32).at[dest].set(flat_tok[order])
    row_w = jnp.zeros((n_rows,), h.dtype).at[dest].set(flat_w[order])
    block_e = jnp.minimum(
        jnp.searchsorted(end_padded, jnp.arange(n_blocks) * MOE_BLOCK, side='right'),
        N_EXPERTS - 1).astype(jnp.int32)
    x_rows = hf[row_tok].reshape(n_blocks, MOE_BLOCK, D)

    def expert_block(args):
        xb, e = args
        a = xb @ w_e_gate[e]
        u = xb @ w_e_up[e]
        return (jax.nn.silu(a) * u) @ w_e_down[e]

    y_rows = lax.map(expert_block, (x_rows, block_e)).reshape(n_rows, D)
    y = jax.ops.segment_sum(y_rows * row_w[:, None], row_tok, num_segments=T)
    return y.reshape(B, S, D)

def first_inputs(seed: int = 0) -> dict:
    key = jax.random.key(seed)
    ks = jax.random.split(key, 20)
    f32 = jnp.float32
    nrm = lambda k, shape, fan: jax.random.normal(k, shape, f32) * (fan ** -0.5)
    return {
        "x": jax.random.normal(ks[0], (BATCH, SEQ, D_MODEL), f32),
        "norm_mix_g": 1.0 + 0.02 * jax.random.normal(ks[1], (D_MODEL,), f32),
        "w_in": nrm(ks[2], (D_MODEL, D_IN_PROJ), D_MODEL),
        "conv_w": nrm(ks[3], (CONV_WIDTH, D_CONV), CONV_WIDTH),
        "conv_b": 0.01 * jax.random.normal(ks[4], (D_CONV,), f32),
        "b_forget": jax.random.uniform(ks[5], (N_HEADS,), f32, 1.0, 6.0),
        "w_conv_out": nrm(ks[6], (D_CONV, D_MODEL), D_CONV),
        "w_att_out": nrm(ks[7], (D_ATT, D_MODEL), D_ATT),
        "w_out": nrm(ks[8], (D_MODEL, D_MODEL), D_MODEL),
        "norm_ffn_g": 1.0 + 0.02 * jax.random.normal(ks[9], (D_MODEL,), f32),
        "w_router_group": nrm(ks[10], (D_MODEL, N_GROUPS), D_MODEL),
        "w_router_expert": nrm(ks[11], (N_GROUPS, D_MODEL, EXPERTS_PER_GROUP), D_MODEL),
        "w_e_gate": nrm(ks[12], (N_EXPERTS, D_MODEL, D_EXPERT), D_MODEL),
        "w_e_up": nrm(ks[13], (N_EXPERTS, D_MODEL, D_EXPERT), D_MODEL),
        "w_e_down": nrm(ks[14], (N_EXPERTS, D_EXPERT, D_MODEL), D_EXPERT),
        "norm_final_g": 1.0 + 0.02 * jax.random.normal(ks[15], (D_MODEL,), f32),
    }

def first_block(x, norm_mix_g, w_in, conv_w, conv_b, b_forget, w_conv_out, w_att_out, w_out,
              norm_ffn_g, w_router_group, w_router_expert, w_e_gate, w_e_up, w_e_down,
              norm_final_g):
    for _ in range(DEPTH):
        x = x + token_mixer(rmsnorm(x, norm_mix_g), w_in, conv_w, conv_b, b_forget,
                            w_conv_out, w_att_out, w_out)
        x = x + hier_moe(rmsnorm(x, norm_ffn_g), w_router_group, w_router_expert,
                         w_e_gate, w_e_up, w_e_down)
    return rmsnorm(x, norm_final_g)


DEPTH_2 = 2

RMS_EPS = 1e-6
M_HEADS = 4
M_HEAD_DIM = D_MODEL // 4
M_WIDTH = M_HEADS * M_HEAD_DIM
CONV_K = 4
P_GROUPS = 4
P_WINDOWS = (2, 4, 8, 16)
P_GROUP_DIM = D_MODEL // 4
P_WIDTH = P_GROUPS * P_GROUP_DIM
A_IN = 3 * M_WIDTH + 2 * M_HEADS + 2 * P_WIDTH
A_OUT_IN = M_WIDTH + P_WIDTH
C_HEADS = 8
QK_NOPE = 128
QK_ROPE = 64
QK_HEAD = QK_NOPE + QK_ROPE
V_HEAD = 128
Q_LORA = 384
KV_LORA = 256
C_WIDTH = C_HEADS * V_HEAD
C_IN = Q_LORA + KV_LORA + QK_ROPE + C_WIDTH
ROPE_THETA = 10000.0
N_A = (DEPTH_2 + 1) // 2
N_C = DEPTH_2 // 2


def rms_norm(x, g):
    xf = x.astype(jnp.float32)
    y = xf * lax.rsqrt(jnp.mean(xf * xf, axis=-1, keepdims=True) + RMS_EPS)
    return (y * g.astype(jnp.float32)).astype(x.dtype)

def causal_conv(x, w, b):
    y = lax.conv_general_dilated(x, w[:, None, :].astype(x.dtype), window_strides=(1,),
                                 padding=[(CONV_K - 1, 0)],
                                 dimension_numbers=('NWC', 'WIO', 'NWC'),
                                 feature_group_count=x.shape[-1])
    return y + b

def mlstm_chunkwise(q, k, v, i_pre, log_f):
    B, H, S, Dk = q.shape
    Dv = v.shape[-1]
    nc = S // CHUNK

    def to_chunks(a):
        return jnp.moveaxis(a.reshape(B, H, nc, CHUNK, *a.shape[3:]), 2, 0)

    xs = (to_chunks(q), to_chunks(k), to_chunks(v), to_chunks(i_pre), to_chunks(log_f))
    tri = jnp.tril(jnp.ones((CHUNK, CHUNK), dtype=bool))

    def step(carry, inp):
        C, n, m = carry
        qb, kb, vb, ib, fb = inp
        bcum = jnp.cumsum(fb, axis=-1)
        dmat = jnp.where(tri, bcum[..., :, None] - bcum[..., None, :] + ib[..., None, :], -jnp.inf)
        inter = bcum + m[..., None]
        m_t = jnp.maximum(inter, jnp.max(dmat, axis=-1))
        w_inter = jnp.exp(inter - m_t)
        s = jnp.einsum('bhtd,bhsd->bhts', qb, kb) * jnp.exp(dmat - m_t[..., None])
        num = jnp.einsum('bhts,bhsv->bhtv', s, vb) + w_inter[..., None] * jnp.einsum('bhtd,bhdv->bhtv', qb, C)
        den = jnp.sum(s, axis=-1) + w_inter * jnp.einsum('bhtd,bhd->bht', qb, n)
        h = num / jnp.maximum(jnp.abs(den), jnp.exp(-m_t))[..., None]
        b_last = bcum[..., -1]
        g = b_last[..., None] - bcum + ib
        m_new = jnp.maximum(b_last + m, jnp.max(g, axis=-1))
        ws = jnp.exp(g - m_new[..., None])
        wc = jnp.exp(b_last + m - m_new)
        kw = kb * ws[..., None]
        C_new = wc[..., None, None] * C + jnp.einsum('bhsd,bhsv->bhdv', kw, vb)
        n_new = wc[..., None] * n + jnp.sum(kw, axis=2)
        return (C_new, n_new, m_new), h

    init = (jnp.zeros((B, H, Dk, Dv), jnp.float32), jnp.zeros((B, H, Dk), jnp.float32),
            jnp.zeros((B, H), jnp.float32))
    _, hs = lax.scan(step, init, xs)
    return jnp.moveaxis(hs, 0, 2).reshape(B, H, S, Dv)

def multiscale_pool(xp):
    B, S, _ = xp.shape
    xf = xp.astype(jnp.float32)
    cs = jnp.pad(jnp.cumsum(xf, axis=1), ((0, 0), (1, 0), (0, 0)))
    t = jnp.arange(S)
    means = []
    for g, w in enumerate(P_WINDOWS):
        csg = cs[..., g * P_GROUP_DIM:(g + 1) * P_GROUP_DIM]
        lo = jnp.maximum(t + 1 - w, 0)
        cnt = jnp.minimum(t + 1, w).astype(jnp.float32)
        means.append((csg[:, 1:] - jnp.take(csg, lo, axis=1)) / cnt[None, :, None])
    return (jnp.concatenate(means, axis=-1) - xf).astype(xp.dtype)

def mlstm_pool_layer(x, norm_g, w_in, b_if, conv_w, conv_b, w_q, w_k, w_v, head_norm_g, skip,
                     pool_w, pool_scale, w_out):
    B, S, _ = x.shape
    u = rms_norm(x, norm_g) @ w_in
    s1 = M_WIDTH
    s2 = 2 * M_WIDTH
    s3 = s2 + 2 * M_HEADS
    s4 = s3 + M_WIDTH
    s5 = s4 + P_WIDTH
    xm, om, gates, zm, xp, zp = jnp.split(u, [s1, s2, s3, s4, s5], axis=-1)
    xc = jax.nn.silu(causal_conv(xm, conv_w, conv_b))
    xc_h = xc.reshape(B, S, M_HEADS, M_HEAD_DIM)
    xm_h = xm.reshape(B, S, M_HEADS, M_HEAD_DIM)
    q = jnp.einsum('bshc,hcd->bhsd', xc_h, w_q).astype(jnp.float32)
    k = jnp.einsum('bshc,hcd->bhsd', xc_h, w_k).astype(jnp.float32) * (M_HEAD_DIM ** -0.5)
    v = jnp.einsum('bshc,hcd->bhsd', xm_h, w_v).astype(jnp.float32)
    gates = (gates + b_if).astype(jnp.float32)
    i_pre = jnp.moveaxis(gates[..., :M_HEADS], -1, 1)
    log_f = jnp.moveaxis(jax.nn.log_sigmoid(gates[..., M_HEADS:]), -1, 1)
    hm = mlstm_chunkwise(q, k, v, i_pre, log_f)
    hm = jnp.moveaxis(hm, 1, 2).reshape(B, S, M_WIDTH).astype(x.dtype) * jax.nn.sigmoid(om)
    hm = rms_norm(hm.reshape(B, S, M_HEADS, M_HEAD_DIM),
                  head_norm_g.reshape(M_HEADS, M_HEAD_DIM)).reshape(B, S, M_WIDTH)
    ya = (hm + skip * xc) * jax.nn.silu(zm)
    mix = multiscale_pool(xp).reshape(B, S, P_GROUPS, P_GROUP_DIM)
    yb = jnp.einsum('bsgc,gcd->bsgd', mix, pool_w).reshape(B, S, P_WIDTH) * pool_scale * jax.nn.silu(zp)
    return x + jnp.concatenate([ya, yb], axis=-1) @ w_out

def rope(x, cos, sin):
    x1, x2 = jnp.split(x.astype(jnp.float32), 2, axis=-1)
    return jnp.concatenate([x1 * cos - x2 * sin, x2 * cos + x1 * sin], axis=-1).astype(x.dtype)

def block_causal_attention(q, k, v):
    B, S, H, _ = q.shape
    scale = QK_HEAD ** -0.5
    chunk_id = jnp.arange(S) // CHUNK
    outs = []
    for qb in range(S // Q_BLOCK):
        q0, q1 = qb * Q_BLOCK, (qb + 1) * Q_BLOCK
        s = jnp.einsum('bqhd,bkhd->bhqk', q[:, q0:q1], k[:, :q1],
                       preferred_element_type=jnp.float32) * scale
        mask = chunk_id[q0:q1, None] >= chunk_id[None, :q1]
        p = jax.nn.softmax(jnp.where(mask, s, -jnp.inf), axis=-1).astype(v.dtype)
        outs.append(jnp.einsum('bhqk,bkhd->bqhd', p, v[:, :q1]))
    return jnp.concatenate(outs, axis=1)

def mla_layer(x, positions, norm_g, w_in, q_norm_g, kv_norm_g, w_uq, w_ukv, qn_g, kn_g, w_out):
    B, S, _ = x.shape
    u = rms_norm(x, norm_g) @ w_in
    cq, ckv, kpe, z = jnp.split(u, [Q_LORA, Q_LORA + KV_LORA, Q_LORA + KV_LORA + QK_ROPE], axis=-1)
    q = (rms_norm(cq, q_norm_g) @ w_uq).reshape(B, S, C_HEADS, QK_HEAD)
    kv = (rms_norm(ckv, kv_norm_g) @ w_ukv).reshape(B, S, C_HEADS, QK_NOPE + V_HEAD)
    k_nope, v = jnp.split(kv, [QK_NOPE], axis=-1)
    k = jnp.concatenate([k_nope, jnp.broadcast_to(kpe[:, :, None, :], (B, S, C_HEADS, QK_ROPE))], axis=-1)
    q = rms_norm(q, qn_g)
    k = rms_norm(k, kn_g)
    inv_freq = ROPE_THETA ** (-jnp.arange(0, QK_ROPE, 2, dtype=jnp.float32) / QK_ROPE)
    ang = positions.astype(jnp.float32)[..., None] * inv_freq
    cos = jnp.cos(ang)[:, :, None, :]
    sin = jnp.sin(ang)[:, :, None, :]
    q = jnp.concatenate([q[..., :QK_NOPE], rope(q[..., QK_NOPE:], cos, sin)], axis=-1)
    k = jnp.concatenate([k[..., :QK_NOPE], rope(k[..., QK_NOPE:], cos, sin)], axis=-1)
    o = block_causal_attention(q, k, v).reshape(B, S, C_WIDTH) * jax.nn.silu(z)
    return x + o @ w_out

def second_inputs(seed: int = 0) -> dict:
    key = jax.random.key(seed)
    ks = list(jax.random.split(key, 32))
    f32 = jnp.float32

    def normal(shape, scale):
        return jax.random.normal(ks.pop(), shape, f32) * scale

    def gain(shape):
        return 1.0 + normal(shape, 0.02)

    x = normal((BATCH, SEQ, D_MODEL), 1.0)
    offsets = jax.random.randint(ks.pop(), (BATCH, 1), 0, 64) * CHUNK
    positions = (offsets + jnp.arange(SEQ)[None, :]).astype(jnp.int32)
    a_b_if = jnp.concatenate([normal((N_A, M_HEADS), 0.1),
                              jnp.linspace(3.0, 6.0, M_HEADS)[None, :] + normal((N_A, M_HEADS), 0.1)], axis=-1)
    return {
        'x': x,
        'positions': positions,
        'a_norm_g': gain((N_A, D_MODEL)),
        'a_w_in': normal((N_A, D_MODEL, A_IN), D_MODEL ** -0.5),
        'a_b_if': a_b_if,
        'a_conv_w': normal((N_A, CONV_K, M_WIDTH), CONV_K ** -0.5),
        'a_conv_b': normal((N_A, M_WIDTH), 0.02),
        'a_w_q': normal((N_A, M_HEADS, M_HEAD_DIM, M_HEAD_DIM), M_HEAD_DIM ** -0.5),
        'a_w_k': normal((N_A, M_HEADS, M_HEAD_DIM, M_HEAD_DIM), M_HEAD_DIM ** -0.5),
        'a_w_v': normal((N_A, M_HEADS, M_HEAD_DIM, M_HEAD_DIM), M_HEAD_DIM ** -0.5),
        'a_head_norm_g': gain((N_A, M_WIDTH)),
        'a_skip': gain((N_A, M_WIDTH)),
        'a_pool_w': normal((N_A, P_GROUPS, P_GROUP_DIM, P_GROUP_DIM), P_GROUP_DIM ** -0.5),
        'a_pool_scale': 1.0 + normal((N_A, P_WIDTH), 0.1),
        'a_w_out': normal((N_A, A_OUT_IN, D_MODEL), A_OUT_IN ** -0.5),
        'c_norm_g': gain((N_C, D_MODEL)),
        'c_w_in': normal((N_C, D_MODEL, C_IN), D_MODEL ** -0.5),
        'c_q_norm_g': gain((N_C, Q_LORA)),
        'c_kv_norm_g': gain((N_C, KV_LORA)),
        'c_w_uq': normal((N_C, Q_LORA, C_HEADS * QK_HEAD), Q_LORA ** -0.5),
        'c_w_ukv': normal((N_C, KV_LORA, C_HEADS * (QK_NOPE + V_HEAD)), KV_LORA ** -0.5),
        'c_qn_g': gain((N_C, QK_HEAD)),
        'c_kn_g': gain((N_C, QK_HEAD)),
        'c_w_out': normal((N_C, C_WIDTH, D_MODEL), C_WIDTH ** -0.5),
    }

def second_block(x, positions, a_norm_g, a_w_in, a_b_if, a_conv_w, a_conv_b, a_w_q, a_w_k, a_w_v,
              a_head_norm_g, a_skip, a_pool_w, a_pool_scale, a_w_out, c_norm_g, c_w_in,
              c_q_norm_g, c_kv_norm_g, c_w_uq, c_w_ukv, c_qn_g, c_kn_g, c_w_out):
    for layer in range(DEPTH_2):
        j = layer // 2
        if layer % 2 == 0:
            x = mlstm_pool_layer(x, a_norm_g[j], a_w_in[j], a_b_if[j], a_conv_w[j], a_conv_b[j],
                                 a_w_q[j], a_w_k[j], a_w_v[j], a_head_norm_g[j], a_skip[j],
                                 a_pool_w[j], a_pool_scale[j], a_w_out[j])
        else:
            x = mla_layer(x, positions, c_norm_g[j], c_w_in[j], c_q_norm_g[j], c_kv_norm_g[j],
                          c_w_uq[j], c_w_ukv[j], c_qn_g[j], c_kn_g[j], c_w_out[j])
    return x


def setup_inputs(seed=0):
    out = dict(first_inputs(seed))
    for name, value in second_inputs(seed + 1).items():
        if name != "x":
            out[name + "_2"] = value
    return out


def reference(
    x, norm_mix_g, w_in, conv_w, conv_b, b_forget, w_conv_out, w_att_out, w_out, norm_ffn_g,
    w_router_group, w_router_expert, w_e_gate, w_e_up, w_e_down, norm_final_g, positions_2,
    a_norm_g_2, a_w_in_2, a_b_if_2, a_conv_w_2, a_conv_b_2, a_w_q_2, a_w_k_2, a_w_v_2,
    a_head_norm_g_2, a_skip_2, a_pool_w_2, a_pool_scale_2, a_w_out_2, c_norm_g_2, c_w_in_2,
    c_q_norm_g_2, c_kv_norm_g_2, c_w_uq_2, c_w_ukv_2, c_qn_g_2, c_kn_g_2, c_w_out_2,
):
    x = first_block(
        x, norm_mix_g, w_in, conv_w, conv_b, b_forget, w_conv_out, w_att_out, w_out, norm_ffn_g,
        w_router_group, w_router_expert, w_e_gate, w_e_up, w_e_down, norm_final_g,
    )
    return second_block(
        x, positions_2, a_norm_g_2, a_w_in_2, a_b_if_2, a_conv_w_2, a_conv_b_2, a_w_q_2,
        a_w_k_2, a_w_v_2, a_head_norm_g_2, a_skip_2, a_pool_w_2, a_pool_scale_2, a_w_out_2,
        c_norm_g_2, c_w_in_2, c_q_norm_g_2, c_kv_norm_g_2, c_w_uq_2, c_w_ukv_2, c_qn_g_2,
        c_kn_g_2, c_w_out_2,
    )


_drawn_inputs = setup_inputs


def setup_inputs(seed=0):
    import zlib

    import numpy as np

    out = dict(_drawn_inputs(seed))
    spreads = {}
    factors = {'conv_b': 3.604,
     'a_norm_g_2': 2.745,
     'a_conv_b_2': 4.515,
     'a_head_norm_g_2': 7.774,
     'a_skip_2': 8.0,
     'c_norm_g_2': 8.0,
     'c_q_norm_g_2': 8.0,
     'c_kv_norm_g_2': 8.0,
     'c_qn_g_2': 8.0,
     'c_kn_g_2': 8.0}
    for name, (base, spread) in spreads.items():
        noise = np.random.default_rng([zlib.crc32(name.encode()), seed]).standard_normal(out[name].shape)
        drawn = base * np.exp(spread * noise) if base else spread * noise
        out[name] = __import__('jax').numpy.asarray(drawn.astype(out[name].dtype))
    for name, factor in factors.items():
        out[name] = (out[name] * factor).astype(out[name].dtype)
    return out
```

```python
from contextlib import ExitStack

import numpy as np

import concourse.bass as bass
from concourse import mybir

F32 = mybir.dt.float32
F32R = mybir.dt.float32r
BF16 = mybir.dt.bfloat16
I32 = mybir.dt.int32
ALU = mybir.AluOpType
ACT = mybir.ActivationFunctionType
AX_X = mybir.AxisListType.X

P = 128
SEQ = 512
D = 1024
TT = SEQ // P
KC = D // P
EPS = 1e-6
MASKED = -1e30

H1, HD1 = 16, 64
NG, EPG = 4, 8
NE = NG * EPG
FE = 512
FC = FE // P
CAP = 64
TOPK = 2
OVF = SEQ * TOPK // CAP - 1
NBLK = NE + OVF + 1

MH, MD = 4, 256
NPOOL = 4
CH, NOPE, ROPE, VH = 8, 128, 64, 128
LAG = 3
QKH = NOPE + ROPE
QL, KVL = 384, 256
HALF = ROPE // 2
C_SCALE = QKH ** -0.5

LO = 32
BASE = 16512
SLICE = 8192
RINGS = 3
BIG = 16384
A0 = BASE + 2 * RINGS * SLICE
MISC = A0 + 8 * BIG

C_ID, C_UP, C_ONE, C_CAUSAL, C_CAUSALT, C_BLOCK, C_IOTA, C_INVF, C_RCNT, C_BACK, C_ROW, C_SPARE, C_END = (
    0, 128, 256, 384, 512, 640, 768, 832, 864, 928, 936, 944, 945)

VECS = ["norm_mix_g", "conv_w0", "conv_w1", "conv_w2", "conv_b", "norm_ffn_g", "a_norm_g", "a_conv_w0",
        "a_conv_w1", "a_conv_w2", "a_conv_w3", "a_conv_b", "a_head_norm_g", "a_skip", "a_pool_scale", "c_norm_g"]
V_QN = len(VECS) * KC
V_KVN = V_QN + QL // P
V_QG = V_KVN + KVL // P
V_KG = V_QG + 1
V_BF = V_KG + 1
V_BI = V_BF + 1
V_BG = V_BI + 1
V_END = V_BG + 1

TWO_PI = (6.28125, 0.0019350051879882812, 3.0199159819e-07)
ROUNDER = 12582912.0


def constants():
    c = np.zeros((P, C_END), np.float32)
    r = np.arange(P)
    c[:, C_ID:C_UP] = np.eye(P)
    c[:, C_UP:C_ONE] = r[:, None] < r[None, :]
    c[:, C_ONE:C_CAUSAL] = 1.0
    c[:, C_CAUSAL:C_CAUSALT] = np.where(r[None, :] > r[:, None], MASKED, 0.0)
    c[:, C_CAUSALT:C_BLOCK] = np.where(r[:, None] > r[None, :], MASKED, 0.0)
    c[:, C_BLOCK:C_IOTA] = np.where(r[None, :] // 64 > r[:, None] // 64, MASKED, 0.0)
    c[:, C_IOTA:C_INVF] = np.arange(CAP)
    c[:, C_BACK:C_ROW] = np.arange(EPG) - 64
    rows = np.arange(TOPK)[:, None] * SEQ + np.arange(TT)[None, :] * P
    c[:, C_ROW:C_SPARE] = rows.reshape(-1)[None, :] + r[:, None] + 1
    c[:, C_SPARE] = TOPK * SEQ + r + 1
    c[:, C_INVF:C_RCNT] = np.float32(10000.0) ** (-np.arange(0, ROPE, 2, dtype=np.float32) / np.float32(ROPE))
    for g in range(NPOOL):
        c[:, C_RCNT + 16 * g:C_RCNT + 16 * g + 16] = 1.0 / np.minimum(np.arange(16) + 1, 2 ** (g + 1))
    return c


def outputs_in_order():
    o = [("hT", 0, j) for j in range(KC)]
    for jj in range(4):
        o += [(n, 2 * jj + a) for n in ("cc", "cu", "cb") for a in range(2)]
    o += [("gconv", j) for j in range(KC)] + [("forget", 0)] + [("conv_out", j) for j in range(KC)]
    o += [("q1", j) for j in range(KC)] + [("k1", j) for j in range(KC)]
    o += [("v1", s, tp) for s in range(4) for tp in range(2)] + [("gatt", j) for j in range(KC)]
    n = H1 * TT
    for i in range(n + LAG + 1):
        o += [("PT1", i - LAG)] * (0 <= i - LAG < n) + [("O1", i - LAG - 1)] * (0 <= i - LAG - 1 < n) + [("S1", i)] * (i < n)
    o += [("OT1", j) for j in range(KC)] + [("att_out", j) for j in range(KC)]
    o += [("mix_out", s, tp) for s in range(4) for tp in range(2)]
    o += [("h2T", j) for j in range(KC)] + [("logits", 0), ("ranks", 0), ("table", 0)]
    o += [("hT", 1, j) for j in range(KC)] + [("xm", j) for j in range(KC)]
    o += [("gates", 0)] + [("om", s, tp) for s in range(4) for tp in range(2)]
    o += [("v2", h, tp) for h in range(MH) for tp in range(2)]
    o += [("q2", j) for j in range(KC)] + [("k2", j) for j in range(KC)] + [("cols", 0)]
    for h in range(MH + 1):
        if h < MH:
            o += [("mrow", h)] + [("ST", h, sb) for sb in range(TT)]
        if h >= 1:
            o += [("num", h - 1, t) for t in range(TT)]
    o += [("zm", j) for j in range(KC)] + [("hmT", j) for j in range(KC)]
    o += [("xp", j) for j in range(KC)] + [("zp", j) for j in range(KC)] + [("pool", j) for j in range(KC)]
    o += [("w_out2", c, t) for c in range(4) for t in range(TT)]
    o += [("hT", 2, j) for j in range(KC)] + [("cin", s, tp) for s in range(3) for tp in range(2)]
    o += [("z3", j) for j in range(KC)] + [("cT", j) for j in range(5)]
    for s in range(5):
        o += [("uq", s, t) for t in range(TT)] * (s < 4)
        o += ([("knT", s - 1, a) for a in range(2)] + [("kpT", s - 1)]) * (s >= 1)
        o += ([("ukv", s, t) for t in range(TT)] + [("qnT", s, a) for a in range(2)] + [("qpT", s)]) * (s < 4)
    n = CH * TT
    for i in range(n + LAG + 1):
        o += [("PT3", i - LAG)] * (0 <= i - LAG < n) + [("O3", i - LAG - 1)] * (0 <= i - LAG - 1 < n) + [("S3", i)] * (i < n)
    o += [("OT3", j) for j in range(KC)] + [("out3", s, tp) for s in range(4) for tp in range(2)]
    return {k: n for n, k in enumerate(o)}


def build_kernel(nc, t):
    with ExitStack() as ctx:
        def at(name, shape, dt, offset):
            return nc.alloc_sbuf_tensor_at(name, shape, dt, offset=offset)

        def big(name, i, dt=F32, shape=(P, KC, SEQ), extra=0):
            return at(name, list(shape), dt, A0 + i * BIG + extra)

        sems = {}

        def sem(name):
            if name not in sems:
                sems[name] = ctx.enter_context(nc.semaphore(name))
            return sems[name]

        bank = [ctx.enter_context(nc.psum_tensor(f"bank{i}", [P, 512], F32)) for i in range(8)]
        raw = [at(f"w_raw{r}", [P, SLICE // 4], F32, BASE + r * SLICE) for r in range(RINGS)]
        w_lo = [at(f"w_lo{r}", [P, SLICE // 4], F32R, BASE + r * SLICE) for r in range(RINGS)]
        w_hi = [at(f"w_hi{r}", [P, SLICE // 4], F32R, BASE + (RINGS + r) * SLICE) for r in range(RINGS)]

        place = [MISC]

        def misc(name, shape, dt):
            size = int(np.prod(shape[1:])) * (2 if dt == BF16 else 4)
            x = at(name, shape, dt, place[0])
            place[0] += -(-size // 32) * 32
            return x

        const = misc("const", [P, C_END], F32)
        vec = misc("vec", [P, V_END], F32)
        id_b = misc("id_b", [P, P], BF16)
        causal_b = misc("causal_b", [P, P], BF16)
        block_b = misc("block_b", [P, P], BF16)
        up_b = misc("up_b", [P, P], BF16)
        ones_b = misc("ones_b", [P, P], BF16)
        pick_r = misc("pick_r", [P, H1], F32R)
        ssq = misc("ssq", [P, 16], F32)
        ssum = misc("ssum", [P, 8], F32)
        r_fin = misc("r_fin", [P, TT], F32)
        var = misc("var", [P, 16], F32)
        root = misc("root", [P, 16], F32)
        rstd = misc("rstd", [P, 16], F32)
        newton = misc("newton", [P, 16], F32)
        neg_max = misc("neg_max", [P, 8], F32)
        row_sum = misc("row_sum", [P, 8], F32)
        inv_sum = misc("inv_sum", [P, 8], F32)
        tok_w = misc("tok_w", [P, 2, TT], F32)
        table = misc("table", [CAP, NBLK, 2], I32)
        get_row = [misc(f"get_row{p}", [CAP, 1], I32) for p in range(2)]
        put_row = [misc(f"put_row{p}", [CAP, 1], I32) for p in range(2)]
        over = misc("over", [P, 32], I32)
        pool_mark = misc("pool_mark", [P, 2], I32)
        pos_i = misc("pos_i", [P, TT], I32)
        pos_f = misc("pos_f", [P, TT], F32)
        mark = misc("mark", [P, 8], F32)
        T0 = place[0]
        assert T0 + 12 * 2048 <= 229344, T0 + 12 * 2048

        def temp(name, i, shape=(P, 512), dt=F32, extra=0):
            return at(name, list(shape), dt, T0 + i * 2048 + extra)

        ident = const[:, C_ID:C_UP]

        def vcol(name, j):
            i = VECS.index(name) * KC + j
            return vec[:, i:i + 1]

        x_tok = big("x_tok", 2, shape=(P, TT, D))
        hT_hi = [big("h1T_hi", 0, F32R), big("h2T_hi", 0, F32R), big("h3T_hi", 2, F32R)]
        hT_lo = [big("h1T_lo", 1, F32R), big("h2T_lo", 1, F32R), big("h3T_lo", 3, F32R)]
        yT_hi, yT_lo = big("yT_hi", 2, F32R), big("yT_lo", 3, F32R)
        mixT = big("mixT", 4)
        q1T, k1T = big("q1T", 2), big("k1T", 3)
        v1 = big("v1", 5, shape=(P, TT, D))
        gattT = big("gattT", 7)
        o1_tok = big("o1_tok", 6, shape=(P, TT, D))
        o1T_hi, o1T_lo = big("o1T_hi", 0, F32R), big("o1T_lo", 1, F32R)
        mixT_hi, mixT_lo = big("mixT_hi", 2, F32R), big("mixT_lo", 3, F32R)
        x1_tok = big("x1_tok", 6, shape=(P, TT, D))
        cc_t = [temp(f"cc_t{p}", p) for p in range(2)]
        z_t = [temp(f"z_t{p}", 2 + p) for p in range(2)]
        acc_t = [temp(f"acc_t{p}", 4 + p) for p in range(2)]
        f_x, f_abs, f_e, f_l = (temp(f"f_{n}", 7 + i, (H1, 512)) for i, n in enumerate("xael"))
        f_one = temp("f_one", 11, (H1, 512))
        neg = temp("neg", 0, dt=F32R)
        p_t = [temp(f"p_t{b}", b) for b in (1, 2, 3, 4)]
        pT_t = [temp(f"pT_t{b}", 5 + b, (P, TT, P)) for b in range(2)]
        ring_gate = [big("gate0", 4), big("gate1", 0)]
        ring_up = [big("up0", 5), big("up1", 1)]
        ring_down = [big("down0", 7, shape=(P, FC, D)), big("down1", 2, shape=(P, FC, D))]
        h2_tok = big("h2_tok", 3, shape=(P, TT, D))
        down_hi = big("down_hi", 3, F32R, (P, FC, D))
        down_lo = [big("down_lo0", 7, F32R, (P, FC, D)), big("down_lo1", 2, F32R, (P, FC, D))]
        hx_hi = [at(f"hx_hi{p}", [P, FC, P], F32R, BASE + 4096 * p) for p in range(2)]
        hx_lo = [at(f"hx_lo{p}", [P, FC, P], F32R, BASE + 4096 * p + 2048) for p in range(2)]
        h2T = at("h2T", [P, KC, SEQ], F32, BASE)
        junk0 = big("junk0", 4, shape=(P, D))
        junk2 = big("junk2", 5, shape=(P, D))
        xg = [at(f"xg{p}", [CAP, D], F32, BASE + 20480 + 4096 * p) for p in range(2)]
        xT = [at(f"xT{p}", [P, KC, CAP], F32, BASE + 28672 + 2048 * p) for p in range(2)]
        sg = [at(f"sg{p}", [P, FC, CAP], F32, BASE + 32768 + 1024 * p) for p in range(2)]
        hx = [at(f"hx{p}", [P, FC, CAP], F32, BASE + 34816 + 1024 * p) for p in range(2)]
        ys = [at(f"ys{p}", [CAP, D], F32, BASE + 36864 + 4096 * p) for p in range(2)]
        w_router = temp("w_router", 0, (P, KC, 36))
        lg = temp("lg", 1, (P, TT, 36))
        les = temp("les", 2, (P, TT, EPG))
        les2 = temp("les2", 2, (P, TT, EPG), extra=256)
        cand = temp("cand", 2, (P, TT, EPG), extra=512)
        one1 = temp("one1", 2, (P, TT, EPG), extra=768)
        one2 = temp("one2", 2, (P, TT, EPG), extra=1024)
        one_g = temp("one_g", 2, (P, TT, NG), extra=1280)
        cand_g = temp("cand_g", 2, (P, TT, NG), extra=1408)
        eg = temp("eg", 2, (P, TT, NG), extra=1536)
        wide = temp("wide", 3, (P, TT, NG, EPG))
        hot = temp("hot", 4, (P, TOPK, TT, NG, EPG))
        hots = temp("hots", 5, (P, TT, NG, EPG), BF16)
        novf, incl, first, ones_e = (temp(n, 5, (P, NE), extra=512 + 128 * i) for i, n in enumerate(("novf", "incl", "first", "ones_e")))
        hot_block = temp("hot_block", 6, (P, TOPK * TT, NBLK))
        hot_slot = temp("hot_slot", 7, (P, TOPK * TT, CAP))
        sm = temp("sm", 8, (P, 24, 8))
        counts = temp("counts", 8, (P, 8 + NE), extra=1024)
        blocks = temp("blocks", 8, (P, 8 + NE), extra=1280)
        slot_r, slot_u, slot_g = (temp(n, 1, (CAP, NBLK), extra=1024 + 192 * i) for i, n in enumerate(("slot_r", "slot_u", "slot_g")))
        ovt = temp("ovt", 9, (P, 16, NE))
        ovs = temp("ovs", 11, (P, 32))
        y1_tok, y2_tok = big("y1_tok", 0, shape=(P, TT, D)), big("y2_tok", 1, shape=(P, TT, D))
        gfin = at("gfin", [P, D], F32, A0 + 4 * BIG)
        x2g_tok = big("x2g_tok", 7, shape=(P, TT, D))
        xmT_hi, xmT_lo = big("xmT_hi", 2, F32R), big("xmT_lo", 3, F32R)
        xcT_hi, xcT_lo = big("xcT_hi", 4, F32R), big("xcT_lo", 5, F32R)
        v2 = big("v2", 7, shape=(P, TT, MH, MD))
        hm_tok = big("hm_tok", 6, shape=(P, TT, MH, MD))
        q2T, k2T = big("q2T", 3), big("k2T", 2)
        zmT = big("zmT", 3)
        ya_hi, ya_lo = big("ya_hi", 2, F32R), big("ya_lo", 7, F32R)
        poolT_hi, poolT_lo = big("poolT_hi", 4, F32R), big("poolT_lo", 5, F32R)
        zpT = big("zpT", 6)
        yb_hi, yb_lo = big("yb_hi", 3, F32R), big("yb_lo", 0, F32R)
        x4_tok = big("x4_tok", 1, shape=(P, TT, D))
        cv_t = [temp(f"cv_t{p}", p) for p in range(2)]
        xs_t = [temp(f"xs_t{p}", 2 + p) for p in range(2)]
        g_i, g_x, g_abs, g_e, g_l, g_one, g_m = (temp(f"g_{n}", 5 + i, (MH, 512)) for i, n in enumerate("ixaelom"))
        neg_m = temp("neg_m", 0, dt=F32R)
        wexp = [temp("wexp0", 2), temp("wexp1", 3)]
        mdiag = temp("mdiag", 4, (P, TT, P))
        sw = [temp(f"sw{p}", 5 + 2 * p, (P, 1280), extra=1024 * p) for p in range(2)]
        cols = temp("cols", 10, (P, 2, TT, MH))
        den_t = temp("den_t", 10, (P, 8), extra=512)
        hsq = temp("hsq", 11, (P, MD))
        hx_t = [temp(f"hx_t{p}", p) for p in range(2)]
        hy_t = [temp(f"hy_t{p}", 2 + p) for p in range(2)]
        px_t = [temp(f"px_t{p}", 4 + p) for p in range(2)]
        ps_t = [temp(f"ps_t{p}", 6 + p) for p in range(2)]
        pm_t = [temp(f"pm_t{p}", 8 + p) for p in range(2)]
        yb_t = [temp(f"yb_t{p}", 10 + p) for p in range(2)]
        c_tok = big("c_tok", 5, shape=(P, TT, QL + KVL + ROPE))
        zT = big("zT", 0)
        cT_hi = big("cT_hi", 4, F32R, (P, 5, SEQ))
        cT_lo = big("cT_lo", 6, F32R, (P, 5, SEQ))
        qb = at("qb", [P, TT, 2, QKH], F32, A0 + 4 * BIG + 10240)
        kb = at("kb", [P, TT, 2, NOPE], F32, A0 + 6 * BIG + 10240)
        qnT, knT = big("qnT", 2, shape=(P, CH, SEQ)), big("knT", 3, shape=(P, CH, SEQ))
        qpT = big("qpT", 7, shape=(P, CH // 2, SEQ))
        kpT = big("kpT", 7, shape=(P, CH // 2, SEQ), extra=8192)
        v3 = big("v3", 5, shape=(P, TT, CH, VH))
        o3_tok = big("o3_tok", 4, shape=(P, TT, D))
        yT3_hi, yT3_lo = big("yT3_hi", 6, F32R), big("yT3_lo", 2, F32R)
        cs_t = temp("cs_t", 0, (P, 2, TT, HALF))
        gr = temp("gr", 1, (P, 2, ROPE))
        qtab = temp("qtab", 2, (P, 4, TT, HALF))
        kpe = temp("kpe", 3, (P, TT, ROPE))
        rp_a = temp("rp_a", 4, (P, TT * 2, HALF))
        rp_b = temp("rp_b", 4, (P, TT * 2, HALF), extra=1024)
        qr = temp("qr", 5, (P, TT, 2, ROPE))
        kr = temp("kr", 6, (P, TT, 2, ROPE))
        rq = temp("rq", 7, (P, TT, CH))
        kpes = temp("kpes", 7, (P, 16), extra=512)
        sq_junk = temp("sq_junk", 11)
        sq_junk2 = temp("sq_junk2", 0)
        diag = temp("diag", 10, (P, TT, P))
        ang = temp("ang", 8, (P, TT, HALF))
        ang_k = temp("ang_k", 8, (P, TT, HALF), extra=512)
        sq_t = [temp("sq_t0", 8, (P, TT, 2, QKH))]
        p3_t = [temp(f"p3_t{b}", b) for b in (1, 2, 3, 4)]
        pT3_t = [temp(f"pT3_t{b}", 5, (P, TT, P)) if b == 0 else temp(f"pT3_t{b}", 8, (P, TT, P)) for b in range(2)]
        y3_t = [temp(f"y3_t{p}", 9 + p) for p in range(2)]
        nb3 = temp("nb3", 11, (P, 8))

        x3_dram = nc.dram_tensor("x3_dram", (SEQ, D), F32).ap()
        h2_dram = nc.dram_tensor("h2_dram", (SEQ, D), F32).ap()
        y_dram = nc.dram_tensor("y_dram", (TOPK * SEQ + CAP, D), F32).ap()
        tok_view = lambda a: a.rearrange("(t p) d -> p t d", p=P)
        x_v = tok_view(t["x"])
        out_v = tok_view(t["out"])

        slices = []
        slice_no = {}

        def add_slice(key, src, parts, cols):
            slice_no[key] = len(slices)
            slices.append((src, parts, cols))

        def cols_of(w, a, n):
            return w.rearrange("(c p) n -> p c n", p=P)[:, :, a:a + n]

        w_in = t["w_in"]
        for jj in range(4):
            for n, name in ((1, "cc"), (2, "cu"), (0, "cb")):
                add_slice((name, jj), cols_of(w_in, n * D + 256 * jj, 256), KC, 256)
        for s in range(4):
            add_slice(("gconv", s), cols_of(w_in, 6 * D + H1 + 256 * s, 256), KC, 256)
        add_slice(("forget", 0), t["w_forget"], KC, P)
        for s in range(4):
            add_slice(("conv_out", s), cols_of(t["w_conv_out"], 256 * s, 256), KC, 256)
        for n, name in ((3, "q1"), (4, "k1"), (5, "v1")):
            for s in range(4):
                add_slice((name, s), cols_of(w_in, n * D + 256 * s, 256), KC, 256)
        for s in range(4):
            add_slice(("gatt", s), cols_of(w_in, 7 * D + H1 + 256 * s, 256), KC, 256)
        for s in range(4):
            add_slice(("att_out", s), cols_of(t["w_att_out"], 256 * s, 256), KC, 256)
        for s in range(4):
            add_slice(("mix_out", s), cols_of(t["w_out"], 256 * s, 256), KC, 256)
        slices1 = len(slices)
        a_in = t["a_w_in"]
        for s in range(4):
            add_slice(("xm", s), cols_of(a_in, 256 * s, 256), KC, 256)
        per_head = lambda w: w.rearrange("h (c p) n -> p (h c) n", p=P)
        add_slice(("gates", 0), t["w_gates"], KC, P)
        for s in range(4):
            add_slice(("om", s), cols_of(a_in, D + 256 * s, 256), KC, 256)
        add_slice(("v2", 0), per_head(t["a_w_v"]), KC, 256)
        add_slice(("q2", 0), per_head(t["a_w_q"]), KC, 256)
        add_slice(("k2", 0), per_head(t["a_w_k"]), KC, 256)
        for n, name in ((0, "zm"), (1, "xp"), (2, "zp")):
            for s in range(4):
                add_slice((name, s), cols_of(a_in, 2 * D + 8 + n * D + 256 * s, 256), KC, 256)
        add_slice(("pool", 0), per_head(t["a_pool_w"]), KC, 256)
        w_o2 = t["a_w_out"].rearrange("(b c p) n -> p b c n", p=P, b=2)
        for c in range(4):
            for b in range(2):
                add_slice(("w_out2", c, b), w_o2[:, b, :, 256 * c:256 * c + 256], KC, 256)
        for s, n in enumerate((256, 256, 192)):
            add_slice(("cin", s), cols_of(t["c_w_in"], 256 * s, n), KC, n)
        for s in range(4):
            add_slice(("z3", s), cols_of(t["c_w_in"], QL + KVL + ROPE + 256 * s, 256), KC, 256)
        for s in range(4):
            add_slice(("uq", s), cols_of(t["c_w_uq"], 2 * QKH * s, 2 * QKH), QL // P, 2 * QKH)
            add_slice(("ukv", s), cols_of(t["c_w_ukv"], 512 * s, 512), KVL // P, 512)
        for s in range(4):
            add_slice(("out3", s), cols_of(t["c_w_out"], 256 * s, 256), KC, 256)
        n_slices = len(slices)

        def ring_view(ring, n):
            _, parts, cols = slices[n]
            return ring[n % RINGS][:, 0:parts * cols].rearrange("p (c n) -> p c n", c=parts)

        last_of = {}
        for (name, *ix), n in ((k, n) for k, n in slice_no.items()):
            s = ix[0]
            last_of[n] = {
                "forget": ("forget", 0), "gates": ("gates", 0), "v2": ("v2", MH - 1, 1), "q2": ("q2", KC - 1),
                "k2": ("k2", KC - 1), "pool": ("pool", KC - 1), "v1": ("v1", s, 1), "mix_out": ("mix_out", s, 1),
                "om": ("om", s, 1), "w_out2": ("w_out2", s, TT - 1), "cin": ("cin", s, 1), "uq": ("uq", s, TT - 1),
                "ukv": ("ukv", s, TT - 1), "out3": ("out3", s, 1)}.get(name, (name, 2 * s + 1))
            if name == "w_out2" and ix[1] == 0:
                last_of[n] = ("half", s)

        order = outputs_in_order()
        results = sem("results")
        drained = [sem(f"drained{b}") for b in range(8)]

        def bank_of(key):
            return bank[order[key] % 8]

        def open_bank(pe, key):
            n = order[key]
            if n >= 8:
                pe.wait_ge(drained[n % 8], n // 8)
            return bank[n % 8]

        def until_made(eng, key):
            eng.wait_ge(results, order[key] + 1)
            return bank_of(key)

        def until_taken(eng, key):
            eng.wait_ge(drained[order[key] % 8], order[key] // 8 + 1)

        def took(ins, key):
            return ins.then_inc(drained[order[key] % 8], 1)

        w_landed = [sem(f"w_landed{r}") for r in range(RINGS)]
        w_hi_made, w_lo_made = sem("w_hi_made"), sem("w_lo_made")
        loaded = sem("loaded")
        x_loaded = [sem(f"x_loaded{tt}") for tt in range(TT)]
        x_back = sem("x_back")
        hi_made = sem("hi_made")
        ssq_made, var_made, root_made, normed = sem("ssq_made"), sem("var_made"), sem("root_made"), sem("normed")
        dve_step, act_step, pool_step = sem("dve_step"), sem("act_step"), sem("pool_step")
        const_made = sem("const_made")
        z_made = sem("z_made")
        h2_stored, x3_stored = sem("h2_stored"), sem("x3_stored")
        gate_landed = [sem(f"gate_landed{p}") for p in range(2)]
        up_landed = [sem(f"up_landed{p}") for p in range(2)]
        down_landed = [sem(f"down_landed{p}") for p in range(2)]
        router_loaded = sem("router_loaded")
        gathered = [sem(f"gathered{p}") for p in range(2)]
        scattered = sem("scattered")
        xt_turned, xt_made, gate_made, up_made = sem("xt_turned"), sem("xt_made"), sem("gate_made"), sem("up_made")
        silu_made, hx_made, y_made, y_taken = sem("silu_made"), sem("hx_made"), sem("y_made"), sem("y_taken")
        down_hi_made, down_lo_made = sem("down_hi_made"), sem("down_lo_made")
        up_half, hx_half = sem("up_half"), sem("hx_half")
        gated_made, hx_hi_made = sem("gated_made"), sem("hx_hi_made")
        turn = sem("turn")
        moe_done, gfin_loaded = sem("moe_done"), sem("gfin_loaded")

        block = ctx.enter_context(nc.Block())

        def over_values(eng):
            eng.wait_ge(sem("over_made"), 1)
            count = eng.value_load(over[0:1, 16:17], min_val=0, max_val=OVF)
            return count, lambda i: eng.value_load(over[0:1, bass.ds(i, 1)], min_val=0, max_val=NE - 1)

        moe_first = order[("hT", 1, 0)]

        def moe_drained(b):
            return len([n for n in range(moe_first) if n % 8 == b])

        @block.sync
        def _(sp):
            def load_slice(n):
                src, _, _ = slices[n]
                if n >= RINGS and n not in range(slices1, slices1 + RINGS):
                    key = last_of[n - RINGS]
                    if key[0] == "half":
                        sp.wait_ge(sem("half_used"), key[1] + 1)
                    else:
                        sp.wait_ge(results, order[key] + 1)
                sp.dma_start(ring_view(raw, n), src).then_inc(w_landed[n % RINGS], 16)

            def load_expert(e, p):
                sp.dma_start(ring_gate[p][:, :, :], gate_src(e)).then_inc(gate_landed[p], 16)
                sp.dma_start(ring_up[p][:, :, :], up_src(e)).then_inc(up_landed[p], 16)
                sp.dma_start(ring_down[p][:, :, :], down_src(e)).then_inc(down_landed[p], 16)

            gate_src = lambda e: t["w_e_gate"][bass.ds(e, 1)].rearrange("e (c p) n -> p (e c) n", p=P)
            up_src = lambda e: t["w_e_up"][bass.ds(e, 1)].rearrange("e (c p) n -> p (e c) n", p=P)
            down_src = lambda e: t["w_e_down"][bass.ds(e, 1)].rearrange("e (c p) n -> p (e c) n", p=P)

            for tt in range(TT):
                sp.dma_start(x_tok[:, tt, :], x_v[:, tt, :]).then_inc(x_loaded[tt], 16)
            for n in range(slices1):
                if n == slice_no[("mix_out", 0)]:
                    until_taken(sp, ("OT1", KC - 1))
                    sp.dma_start(x1_tok[:, :, :], x_v).then_inc(x_back, 16)
                load_slice(n)
            sp.dma_start(w_router[:, :, :], t["w_router"]).then_inc(router_loaded, 16)
            until_taken(sp, ("att_out", KC - 1))
            load_expert(0, 0)
            sp.wait_ge(results, order[("mix_out", 3, 1)] + 1)
            load_expert(1, 1)
            for tt in range(TT):
                sp.wait_ge(sem("h2_rows"), tt + 1)
                sp.dma_start(h2_dram[tt * P:(tt + 1) * P, :], h2_tok[:, tt, :]).then_inc(h2_stored, 16)
            with sp.Fori(1, NE // 2) as i:
                for p in range(2):
                    sp.wait_ge(gate_made, i * 2 + (p - 1))
                    sp.dma_start(ring_gate[p][:, :, :], gate_src(i * 2 + p)).then_inc(gate_landed[p], 16)
                    sp.wait_ge(up_made, i * 2 + (p - 1))
                    sp.dma_start(ring_up[p][:, :, :], up_src(i * 2 + p)).then_inc(up_landed[p], 16)
                    sp.wait_ge(y_made, i * 2 + (p - 1))
                    sp.dma_start(ring_down[p][:, :, :], down_src(i * 2 + p)).then_inc(down_landed[p], 16)
            count, expert_of = over_values(sp)
            with sp.If(count > 0):
                with sp.Fori(0, OVF) as i:
                    with sp.If(count > i):
                        sp.wait_ge(sem("ovf_free"), i + 1)
                        e = expert_of(i)
                        sp.dma_start(ring_gate[0][:, :, :], gate_src(e)).then_inc(sem("ovf_gate"), 16)
                        sp.dma_start(ring_up[0][:, :, :], up_src(e)).then_inc(sem("ovf_up"), 16)
                        sp.dma_start(ring_down[0][:, :, :], down_src(e)).then_inc(sem("ovf_down"), 16)
            sp.wait_ge(moe_done, 1)
            sp.dma_start(gfin[:, :], t["norm_final_g"].unsqueeze(0).to_broadcast([P, D])).then_inc(gfin_loaded, 16)
            y_v = y_dram[0:TOPK * SEQ, :].rearrange("(k t p) d -> k p t d", k=TOPK, p=P)
            for tt in range(TT):
                sp.dma_start(y1_tok[:, tt, :], y_v[0, :, tt, :]).then_inc(sem(f"y_loaded{tt}"), 16)
                sp.dma_start(y2_tok[:, tt, :], y_v[1, :, tt, :]).then_inc(sem(f"y_loaded{tt}"), 16)
                if tt == 0:
                    load_slice(slices1)
            for n in range(slices1 + 1, slices1 + RINGS):
                load_slice(n)
            for tt in range(TT):
                sp.wait_ge(sem("x3_made"), tt + 1)
                sp.dma_start(x3_dram[tt * P:(tt + 1) * P, :], x1_tok[:, tt, :]).then_inc(x3_stored, 16)
            first3 = slice_no[("w_out2", 0, 0)]
            for n in range(slices1 + RINGS, n_slices):
                load_slice(n)
                if n == first3:
                    until_taken(sp, ("zp", KC - 1))
                    sp.wait_ge(x3_stored, 16 * TT)
                    sp.dma_start(x4_tok[:, :, :], tok_view(x3_dram)).then_inc(sem("x3_back"), 16)
                    for k, g in enumerate(("c_qn_rope_g", "c_kn_rope_g")):
                        sp.dma_start(gr[:, k, :], t[g].unsqueeze(0).to_broadcast([P, ROPE])).then_inc(sem("gr_loaded"), 16)
            for s in range(4):
                for tp in range(2):
                    until_taken(sp, ("out3", s, tp))
                sp.dma_start(out_v[:, :, 256 * s:256 * s + 256],
                             x4_tok[:, :, 256 * s:256 * s + 256]).then_inc(sem("stored"), 16)
            sp.wait_ge(sem("stored"), 64)

        @block.gpsimd
        def _(pool):
            steps = [0]

            def step(ins):
                steps[0] += 1
                ins.then_inc(pool_step, 1)
                pool.wait_ge(pool_step, steps[0])

            pool.wait_ge(results, order[("mix_out", 3, 1)] + 1)
            for p in range(2):
                step(nc.gpsimd.memset(ys[p][:, :], 0.0))
                pool.dma_start(y_dram[TOPK * SEQ:, :], ys[p][:, :]).then_inc(scattered, 16)
                pool.wait_ge(scattered, 16 * (p + 1))
            pool.wait_ge(sem("table_made"), 1)
            pool.wait_ge(h2_stored, 16 * TT)
            pool.wait_ge(results, order[("logits", 0)] + 1)

            def gather(p):
                pool.indirect_dma_start(out=xg[p][:, :], out_offset=None, in_=h2_dram,
                                        in_offset=bass.IndirectOffsetOnAxis(ap=get_row[p][:, :], axis=0)).then_inc(gathered[p], 16)

            def scatter(p):
                pool.indirect_dma_start(out=y_dram, out_offset=bass.IndirectOffsetOnAxis(ap=put_row[p][:, :], axis=0),
                                        in_=ys[p][:, :], in_offset=None).then_inc(scattered, 16)

            for p in range(2):
                step(nc.gpsimd.tensor_copy(get_row[p][:, :], table[:, p, 0:1]))
                gather(p)
            base = steps[0]
            with pool.Fori(0, NE // 2) as i:
                for p in range(2):
                    pool.wait_ge(xt_turned, i * 2 + (p + 1))
                    pool.sem_inc(turn, 1)
                    nc.gpsimd.tensor_copy(get_row[p][:, :], table[:, bass.ds(i * 2 + (p + 2), 1), 0]).then_inc(pool_step, 1)
                    pool.wait_ge(pool_step, i * 4 + (base + 2 * p + 1))
                    pool.sem_inc(turn, 1)
                    gather(p)
                    pool.wait_ge(y_taken, i * 2 + (p + 2))
                    pool.sem_inc(turn, 1)
                    pool.wait_ge(scattered, i * 32 + (32 + 16 * p))
                    pool.sem_inc(turn, 1)
                    nc.gpsimd.tensor_copy(put_row[p][:, :], table[:, bass.ds(i * 2 + p, 1), 1]).then_inc(pool_step, 1)
                    pool.wait_ge(pool_step, i * 4 + (base + 2 * p + 2))
                    pool.sem_inc(turn, 1)
                    scatter(p)
            for p in range(2):
                pool.wait_ge(gathered[p], 16 * (NE // 2 + 1))
            pool.wait_ge(scattered, 16 * (NE + 2))
            steps[0] = base + 4 * (NE // 2)
            pool.wait_ge(xt_turned, NE + 1)
            pool.wait_ge(xt_made, NE + 1)
            pool.wait_ge(y_made, NE)
            nc.gpsimd.memset(pool_mark[:, 0:1], 0).then_inc(sem("ovf_free"), 1)
            count, _ = over_values(pool)
            with pool.If(count > 0):
                with pool.Fori(0, OVF) as i:
                    with pool.If(count > i):
                        pool.wait_ge(sem("ovf_free"), i + 1)
                        pool.sem_inc(turn, 1)
                        nc.gpsimd.tensor_copy(get_row[0][:, :], table[:, bass.ds(i + NE, 1), 0]).then_inc(sem("ovf_rows"), 1)
                        pool.wait_ge(sem("ovf_rows"), i * 2 + 1)
                        pool.sem_inc(turn, 1)
                        nc.gpsimd.tensor_copy(put_row[0][:, :], table[:, bass.ds(i + NE, 1), 1]).then_inc(sem("ovf_rows"), 1)
                        pool.wait_ge(sem("ovf_rows"), i * 2 + 2)
                        pool.sem_inc(turn, 1)
                        pool.indirect_dma_start(out=xg[0][:, :], out_offset=None, in_=h2_dram,
                                                in_offset=bass.IndirectOffsetOnAxis(ap=get_row[0][:, :], axis=0)).then_inc(sem("ovf_x"), 16)
                        pool.wait_ge(sem("ovf_ys"), i + 1)
                        pool.sem_inc(turn, 1)
                        pool.indirect_dma_start(out=y_dram, out_offset=bass.IndirectOffsetOnAxis(ap=put_row[0][:, :], axis=0),
                                                in_=ys[0][:, :], in_offset=None).then_inc(sem("ovf_out"), 16)
                        pool.wait_ge(sem("ovf_out"), i * 16 + 16)
                        pool.sem_inc(turn, 1)
                        nc.gpsimd.tensor_copy(put_row[1][:, :], put_row[0][:, :]).then_inc(sem("ovf_free"), 1)
            nc.gpsimd.memset(pool_mark[:, 1:2], 0).then_inc(moe_done, 1)
            for j in range(KC):
                pool.wait_ge(sem("xc_hi"), j + 1)
                nc.gpsimd.tensor_tensor(xcT_lo[:, j, :], xs_t[j % 2][:, :], xcT_hi[:, j, :].bitcast(F32), ALU.subtract)\
                    .then_inc(sem("xc_lo"), 1)
            for j in range(KC):
                if j == 0:
                    until_taken(pool, ("num", MH - 1, TT - 1))
                if j >= 2:
                    pool.wait_ge(sem("ya_made"), j - 1)
                nc.gpsimd.tensor_tensor(hx_t[j % 2][:, :], xcT_hi[:, j, :].bitcast(F32), xcT_lo[:, j, :].bitcast(F32), ALU.add)\
                    .then_inc(sem("xc_again"), 1)

        @block.scalar
        def _(act):
            steps, his, ssqs, roots, vars_ = [0], [0], [0], [0], [0]

            def step(ins):
                steps[0] += 1
                ins.then_inc(act_step, 1)
                act.wait_ge(act_step, steps[0])

            def copy(out, in_, scale=1.0):
                return nc.scalar.activation(out, in_, ACT.Copy, scale=scale)

            def split(n, end):
                if n >= end:
                    return
                act.wait_ge(w_landed[n % RINGS], 16 * (n // RINGS + 1))
                copy(ring_view(w_hi, n), ring_view(raw, n)).then_inc(w_hi_made, 1)

            def evict_hi(key, hi, scale=1.0):
                src = until_made(act, key)
                copy(hi, src[:, :], scale).then_inc(hi_made, 1)

            def squares(src, out, col):
                if ssqs[0]:
                    act.wait_ge(ssq_made, ssqs[0])
                ssqs[0] += 1
                nc.scalar.activation(out, src, ACT.Square, accum_out=ssq[:, col:col + 1]).then_inc(ssq_made, 1)

            def take_root(n):
                vars_[0] += 1
                act.wait_ge(var_made, vars_[0])
                nc.scalar.activation(root[:, 0:n], var[:, 0:n], ACT.Sqrt).then_inc(root_made, 1)

            nc.scalar.dma_start(const[:, :], t["consts"]).then_inc(loaded, 16)
            nc.scalar.dma_start(vec[:, :], t["vecs"]).then_inc(loaded, 16)
            nc.scalar.dma_start(pos_i[:, :], t["positions"]).then_inc(loaded, 16)
            for tt in range(TT):
                act.wait_ge(x_loaded[tt], 16)
                squares(x_tok[:, tt, :], junk0[:, :], tt)
            take_root(TT)
            split(0, slices1)
            act.wait_ge(loaded, 48)
            copy(id_b[:, :], ident).then_inc(const_made, 1)
            copy(causal_b[:, :], const[:, C_CAUSAL:C_CAUSALT]).then_inc(const_made, 1)
            copy(block_b[:, :], const[:, C_BLOCK:C_IOTA]).then_inc(const_made, 1)
            copy(up_b[:, :], const[:, C_UP:C_ONE]).then_inc(const_made, 1)
            copy(ones_b[:, :], const[:, C_ONE:C_CAUSAL]).then_inc(const_made, 1)
            for j in range(KC):
                evict_hi(("hT", 0, j), hT_hi[0][:, j, :], vcol("norm_mix_g", j))
            split(1, slices1)
            for jj in range(4):
                n = slice_no[("cc", jj)]
                for a in range(2):
                    j = 2 * jj + a
                    src = until_made(act, ("cc", j))
                    if j >= 2:
                        act.wait_ge(z_made, j - 1)
                    took(copy(cc_t[j % 2][:, :], src[:, :]), ("cc", j))
                for k in range(3):
                    split(n + 2 + k, slices1)
            for s in range(4):
                for j in (2 * s, 2 * s + 1):
                    src = until_made(act, ("gconv", j))
                    took(nc.scalar.activation(mixT[:, j, :], src[:, :], ACT.Sigmoid), ("gconv", j))
                split(slice_no[("gconv", s)] + 2, slices1)
            until_made(act, ("forget", 0))
            split(slice_no[("forget", 0)] + 2, slices1)
            for s in range(4):
                until_made(act, ("conv_out", 2 * s + 1))
                split(slice_no[("conv_out", s)] + 2, slices1)
                if s == 0:
                    act.wait_ge(sem("f_abs_made"), 1)
                    step(nc.scalar.activation(f_e[:, :], f_abs[:, :], ACT.Exp, scale=-1.0))
                    nc.scalar.activation(f_l[:, :], f_e[:, :], ACT.Ln, bias=1.0).then_inc(sem("f_log_made"), 1)
            for name, dst, scale in (("q1", q1T, HD1 ** -0.5), ("k1", k1T, 1.0)):
                for s in range(4):
                    for j in (2 * s, 2 * s + 1):
                        src = until_made(act, (name, j))
                        took(copy(dst[:, j, :], src[:, :], scale), (name, j))
                    split(slice_no[(name, s)] + 2, slices1)
            for s in range(4):
                for tp in range(2):
                    src = until_made(act, ("v1", s, tp))
                    took(copy(v1[:, 2 * tp:2 * tp + 2, 256 * s:256 * s + 256],
                              src[:, :].rearrange("p (t n) -> p t n", t=2)), ("v1", s, tp))
                split(slice_no[("v1", s)] + 2, slices1)
            for s in range(4):
                for j in (2 * s, 2 * s + 1):
                    src = until_made(act, ("gatt", j))
                    took(nc.scalar.activation(gattT[:, j, :], src[:, :], ACT.Sigmoid), ("gatt", j))
                split(slice_no[("gatt", s)] + 2, slices1)

            def attention(n_items, S, PT, O, p_buf, pT_buf, bias_made, scale):
                for i in range(n_items + LAG):
                    k = i - LAG
                    if k >= 0 and k % 2 == 0:
                        keys = (k % TT + 1) * P
                        src = until_made(act, (PT, k))
                        if k >= 2:
                            act.wait_ge(results, order[(O, k - 2)] + 1)
                        took(copy(pT_buf[k % 2][:, 0:k % TT + 1, :], src[:, 0:keys].rearrange("p (k q) -> p k q", q=P)), (PT, k))
                    if i < n_items:
                        keys = (i % TT + 1) * P
                        act.wait_ge(bias_made, i + 1)
                        if i >= 4:
                            act.wait_ge(results, order[(PT, i - 4)] + 1)
                        if i >= 8:
                            until_taken(act, (O, i - 8))
                        s_, b_ = scale(i)
                        took(nc.scalar.activation(p_buf[i % 4][:, 0:keys], bank_of((S, i))[:, 0:keys], ACT.Exp,
                                                  bias=b_, scale=s_, accum_out=row_sum[:, i % 8:i % 8 + 1]), (S, i))

            attention(H1 * TT, "S1", "PT1", "O1", p_t, pT_t, sem("max1_made"),
                      lambda i: (1.0, neg_max[:, i % 8:i % 8 + 1]))
            for j in range(KC):
                evict_hi(("OT1", j), o1T_hi[:, j, :])
            for s in range(4):
                until_made(act, ("att_out", 2 * s + 1))
                split(slice_no[("att_out", s)] + 2, slices1)
            for s in range(4):
                for tp in range(2):
                    until_taken(act, ("mix_out", s, tp))
                    for tt in (2 * tp, 2 * tp + 1):
                        squares(x1_tok[:, tt, 256 * s:256 * s + 256], sq_junk[:, 0:256], tt * 4 + s)
                split(slice_no[("mix_out", s)] + 2, slices1)
            take_root(TT)
            for j in range(KC):
                src = until_made(act, ("h2T", j))
                took(copy(h2T[:, j, :], src[:, :], vcol("norm_ffn_g", j)), ("h2T", j))
            for tt in range(TT):
                copy(h2_tok[:, tt, :], x1_tok[:, tt, :], rstd[:, tt:tt + 1]).then_inc(sem("h2_rows"), 1)
            act.wait_ge(sem("router_e1"), 1)
            nc.scalar.activation(eg[:, :, :], cand_g[:, :, :], ACT.Exp).then_inc(sem("router_e2"), 1)
            act.wait_ge(sem("router_e3"), 1)
            nc.scalar.activation(sm[:, 6, 0:4], sm[:, 5, 0:4], ACT.Exp).then_inc(sem("router_e4"), 1)
            for b in range(8):
                act.wait_ge(drained[b], moe_drained(b))
            nc.scalar.activation(mark[:, 0:1], const[:, C_ONE:C_ONE + 1], ACT.Copy).then_inc(y_taken, 1)
            act.wait_ge(h2_stored, 16 * TT)
            with act.Fori(0, NE // 2) as i:
                for p in range(2):
                    act.wait_ge(down_landed[p], i * 16 + 16)
                    copy(down_hi[:, :, :], ring_down[p][:, :, :]).then_inc(down_hi_made, 1)
                    act.wait_ge(gate_made, i * 2 + (p + 1))
                    nc.scalar.activation(sg[p][:, :, :], bank[2 + p][:, 0:FC * CAP].rearrange("p (f c) -> p f c", f=FC),
                                         ACT.Silu).then_inc(silu_made, 1)
                    act.wait_ge(y_made, i * 2 + (p + 1))
                    act.wait_ge(scattered, i * 32 + (16 + 16 * p))
                    copy(ys[p][:, 0:512], bank[6][0:CAP, :])
                    copy(ys[p][:, 512:1024], bank[7][0:CAP, :]).then_inc(y_taken, 1)
            count, _ = over_values(act)
            with act.If(count > 0):
                with act.Fori(0, OVF) as i:
                    with act.If(count > i):
                        act.wait_ge(sem("ovf_gate_made"), i + 1)
                        nc.scalar.activation(sg[0][:, :, :], bank[2][:, 0:FC * CAP].rearrange("p (f c) -> p f c", f=FC),
                                             ACT.Silu).then_inc(sem("ovf_silu"), 1)
                        act.wait_ge(sem("ovf_y_made"), i + 1)
                        copy(ys[0][:, 0:512], bank[6][0:CAP, :])
                        copy(ys[0][:, 512:1024], bank[7][0:CAP, :]).then_inc(sem("ovf_ys"), 1)
            act.wait_ge(moe_done, 1)
            for tt in range(TT):
                act.wait_ge(sem("x2_made"), 2 * tt + 1)
                squares(x1_tok[:, tt, :], junk2[:, :], tt)
                act.wait_ge(sem("x2_made"), 2 * tt + 2)
                squares(x2g_tok[:, tt, :], junk2[:, :], TT + tt)
                if tt == 1:
                    split(slices1, n_slices)
            take_root(TT)
            take_root(TT)
            for j in range(KC):
                evict_hi(("hT", 1, j), hT_hi[1][:, j, :], vcol("a_norm_g", j))
            split(slices1 + 1, n_slices)
            act.wait_ge(sem("r_fin_made"), 1)
            for tt in range(TT):
                copy(x1_tok[:, tt, :], x2g_tok[:, tt, :], r_fin[:, tt:tt + 1]).then_inc(sem("x3_made"), 1)
            for s in range(4):
                for j in (2 * s, 2 * s + 1):
                    evict_hi(("xm", j), xmT_hi[:, j, :])
                    until_taken(act, ("xm", j))
                    if j >= 2:
                        act.wait_ge(sem("xc_lo"), j - 1)
                    step(nc.scalar.activation(xs_t[j % 2][:, :], cv_t[j % 2][:, :], ACT.Silu))
                    copy(xcT_hi[:, j, :], xs_t[j % 2][:, :]).then_inc(sem("xc_hi"), 1)
                    if j == 2 * s:
                        split(slice_no[("xm", s)] + 2, n_slices)
            split(slice_no[("gates", 0)] + 2, n_slices)
            act.wait_ge(sem("g_abs_made"), 1)
            step(nc.scalar.activation(g_e[:, :], g_abs[:, :], ACT.Exp, scale=-1.0))
            nc.scalar.activation(g_l[:, :], g_e[:, :], ACT.Ln, bias=1.0).then_inc(sem("g_log_made"), 1)
            for s in range(4):
                for tp in range(2):
                    src = until_made(act, ("om", s, tp))
                    if s == 0:
                        act.wait_ge(x3_stored, 16 * TT)
                    took(nc.scalar.activation(hm_tok[:, 2 * tp:2 * tp + 2, s, :], src[:, :].rearrange("p (t n) -> p t n", t=2),
                                              ACT.Sigmoid), ("om", s, tp))
                split(slice_no[("om", s)] + 2, n_slices)
                if s == 0:
                    act.wait_ge(sem("g_m_made"), 1)
                    nc.scalar.activation(g_e[:, :], g_abs[:, :], ACT.Exp, scale=-1.0).then_inc(sem("g_em_made"), 1)
            for h in range(MH):
                for tp in range(2):
                    src = until_made(act, ("v2", h, tp))
                    took(copy(v2[:, 2 * tp:2 * tp + 2, h, :], src[:, :].rearrange("p (t n) -> p t n", t=2)), ("v2", h, tp))
            split(slice_no[("v2", 0)] + 2, n_slices)
            for name, dst, scale in (("q2", q2T, 1.0), ("k2", k2T, MD ** -0.5)):
                for j in range(KC):
                    src = until_made(act, (name, j))
                    took(copy(dst[:, j, :], src[:, :], scale), (name, j))
                split(slice_no[(name, 0)] + 2, n_slices)
            for h in range(MH):
                src = until_made(act, ("mrow", h))
                act.wait_ge(sem("mdiag_made"), h + 1)
                for sb in range(TT):
                    k = h * TT + sb
                    a_col = cols[:, 0, sb, h:h + 1]
                    if k == 0:
                        until_taken(act, ("cols", 0))
                    if k >= 2:
                        until_taken(act, ("ST", (k - 2) // TT, (k - 2) % TT))
                    ins = nc.scalar.activation(wexp[k % 2][:, 0:P], mdiag[:, sb, :], ACT.Exp, bias=a_col)
                    if sb < TT - 1:
                        ins = nc.scalar.activation(wexp[k % 2][:, P:(TT - sb) * P], src[:, (sb + 1) * P:SEQ], ACT.Exp, bias=a_col)
                    ins.then_inc(sem("wexp_made"), 1)
            until_taken(act, ("num", MH - 1, TT - 1))
            for tt in range(TT):
                for h in range(MH):
                    until_taken(act, ("num", h, tt))
                    squares(hm_tok[:, tt, h, :], hsq[:, :], tt * MH + h)
            take_root(TT * MH)
            for s in range(4):
                for j in (2 * s, 2 * s + 1):
                    src = until_made(act, ("zm", j))
                    took(nc.scalar.activation(zmT[:, j, :], src[:, :], ACT.Silu), ("zm", j))
                split(slice_no[("zm", s)] + 2, n_slices)
            for j in range(KC):
                act.wait_ge(sem("ya_made"), j + 1)
                copy(ya_hi[:, j, :], hy_t[j % 2][:, :]).then_inc(hi_made, 1)
                if j == 3:
                    until_made(act, ("xp", 1))
                    split(slice_no[("xp", 0)] + 2, n_slices)
            until_made(act, ("xp", 3))
            split(slice_no[("xp", 1)] + 2, n_slices)
            for s in range(4):
                for j in (2 * s, 2 * s + 1):
                    src = until_made(act, ("xp", j))
                    if j >= 2:
                        act.wait_ge(sem("mean_made"), j - 1)
                    took(copy(px_t[j % 2][:, :], src[:, :]), ("xp", j))
                name, k = (("xp", 2), ("xp", 3), ("zp", 0), ("zp", 1))[s]
                until_made(act, (name, 2 * k + 1))
                split(slice_no[(name, k)] + 2, n_slices)
            for s in range(4):
                for j in (2 * s, 2 * s + 1):
                    src = until_made(act, ("zp", j))
                    took(nc.scalar.activation(zpT[:, j, :], src[:, :], ACT.Silu), ("zp", j))
                if s >= 2:
                    split(slice_no[("zp", s)] + 2, n_slices)
            until_made(act, ("pool", KC - 1))
            split(slice_no[("pool", 0)] + 2, n_slices)
            for c in range(4):
                split(slice_no[("w_out2", c, 0)] + 2, n_slices)
                act.wait_ge(sem("half_used"), c + 1)
                split(slice_no[("w_out2", c, 0)] + 3, n_slices)
                for tt in range(TT):
                    until_taken(act, ("w_out2", c, tt))
                    squares(x4_tok[:, tt, 256 * c:256 * c + 256], sq_junk2[:, 0:256], tt * 4 + c)
            take_root(TT)
            for j in range(KC):
                evict_hi(("hT", 2, j), hT_hi[2][:, j, :], vcol("c_norm_g", j))
            for s, n in enumerate((256, 256, 192)):
                for tp in range(2):
                    src = until_made(act, ("cin", s, tp))
                    took(copy(c_tok[:, 2 * tp:2 * tp + 2, 256 * s:256 * s + n],
                              src[:, 0:2 * n].rearrange("p (t n) -> p t n", t=2)), ("cin", s, tp))
                split(slice_no[("cin", s)] + 2, n_slices)
            for s in range(3):
                for tp in range(2):
                    until_taken(act, ("cin", s, tp))
            for tt in range(TT):
                squares(c_tok[:, tt, 0:QL], sq_junk[:, 0:QL], tt)
                squares(c_tok[:, tt, QL:QL + KVL], sq_junk[:, 0:KVL], TT + tt)
                squares(c_tok[:, tt, QL + KVL:], sq_junk[:, 0:ROPE], 2 * TT + tt)
            take_root(2 * TT)
            act.wait_ge(sem("angle_made"), 1)
            nc.scalar.activation(cs_t[:, 1, :, :], ang[:, :, :], ACT.Sin).then_inc(sem("sines"), 1)
            act.wait_ge(sem("angle_made"), 2)
            nc.scalar.activation(cs_t[:, 0, :, :], ang_k[:, :, :], ACT.Sin).then_inc(sem("sines"), 1)
            for s in range(4):
                for j in (2 * s, 2 * s + 1):
                    src = until_made(act, ("z3", j))
                    took(nc.scalar.activation(zT[:, j, :], src[:, :], ACT.Silu), ("z3", j))
                split(slice_no[("z3", s)] + 2, n_slices)
            for j in range(5):
                evict_hi(("cT", j), cT_hi[:, j, :], vec[:, V_QN + j:V_QN + j + 1])
            def turned(key, dst, gain=1.0):
                src = until_made(act, key)
                took(copy(dst, src[:, :], gain), key)

            def evict_k(s):
                turned(("knT", s, 0), knT[:, 2 * s, :], vec[:, V_KG:V_KG + 1])
                turned(("knT", s, 1), knT[:, 2 * s + 1, :], vec[:, V_KG:V_KG + 1])
                turned(("kpT", s), kpT[:, s, :])

            for s in range(4):
                if s >= 1:
                    until_taken(act, ("qnT", s - 1, 1))
                    act.wait_ge(sem("q_roped"), s)
                for tt in range(TT):
                    src = until_made(act, ("uq", s, tt))
                    took(copy(qb[:, tt, :, :], src[:, 0:2 * QKH].rearrange("p (h n) -> p h n", h=2)), ("uq", s, tt))
                split(slice_no[("uq", s)] + 2, n_slices)
                for tt in range(TT):
                    until_taken(act, ("uq", s, tt))
                if s >= 1:
                    act.wait_ge(sem("sq_used"), 2 * s)
                nc.scalar.activation(sq_t[0][:, :, :, :], qb[:, :, :, :], ACT.Square).then_inc(sem("sq_made"), 1)
                if s >= 1:
                    evict_k(s - 1)
                for tt in range(TT):
                    src = until_made(act, ("ukv", s, tt))
                    kv = src[:, :].rearrange("p (h n) -> p h n", h=2)
                    step(copy(kb[:, tt, :, :], kv[:, :, 0:NOPE]))
                    took(copy(v3[:, tt, 2 * s:2 * s + 2, :], kv[:, :, NOPE:]), ("ukv", s, tt))
                split(slice_no[("ukv", s)] + 2, n_slices)
                act.wait_ge(sem("sq_used"), 2 * s + 1)
                nc.scalar.activation(sq_t[0][:, :, :, 0:NOPE], kb[:, :, :, :], ACT.Square).then_inc(sem("sq_made"), 1)
                take_root(16)
                turned(("qnT", s, 0), qnT[:, 2 * s, :], vec[:, V_QG:V_QG + 1])
                turned(("qnT", s, 1), qnT[:, 2 * s + 1, :], vec[:, V_QG:V_QG + 1])
                turned(("qpT", s), qpT[:, s, :])
            evict_k(3)
            attention(CH * TT, "S3", "PT3", "O3", p3_t, pT3_t, sem("max3_made"),
                      lambda i: (rq[:, i % TT, i // TT:i // TT + 1], nb3[:, i % 8:i % 8 + 1]))
            for j in range(KC):
                until_taken(act, ("OT3", j))
                copy(yT3_hi[:, j, :], y3_t[j % 2][:, :]).then_inc(hi_made, 1)
            for s in range(4):
                until_made(act, ("out3", s, 1))
                split(slice_no[("out3", s)] + 2, n_slices)

        @block.tensor
        def _(pe):
            def parts3(out, sh, sl, mh, ml, start, stop):
                pe.matmul(out, sh, mh, start=start, stop=False)
                pe.matmul(out, sh, ml, start=False, stop=False)
                return pe.matmul(out, sl, mh, start=False, stop=stop)

            def weights(n):
                pe.wait_ge(w_hi_made, n + 1)
                pe.wait_ge(w_lo_made, n + 1)
                return ring_view(w_hi, n), ring_view(w_lo, n)

            def feature_major(name, s, key, xh, xl, ready=None):
                wh, wl = weights(slice_no[(name, s)])
                for a in range(2):
                    k = key(2 * s + a)
                    out = open_bank(pe, k)
                    for c in range(KC):
                        if ready and s == 0 and a == 0:
                            ready(c)
                        ins = parts3(out[:, :], wh[:, c, a * P:(a + 1) * P], wl[:, c, a * P:(a + 1) * P],
                                     xh[:, c, :], xl[:, c, :], c == 0, c == KC - 1)
                    ins.then_inc(results, 1)

            def token_major(name, s, n, xh, xl, ready=None):
                wh, wl = weights(slice_no[(name, s)])
                for tp in range(2):
                    out = open_bank(pe, (name, s, tp))
                    for a in range(2):
                        tk = slice((2 * tp + a) * P, (2 * tp + a + 1) * P)
                        for c in range(KC):
                            if ready and s == 0 and tp == 0 and a == 0:
                                ready(c)
                            ins = parts3(out[:, a * n:(a + 1) * n], xh[:, c, tk], xl[:, c, tk], wh[:, c, :], wl[:, c, :],
                                         c == 0, c == KC - 1)
                    ins.then_inc(results, 1)

            def chunk_taken(name, *rest):
                return lambda c: until_taken(pe, (name, *rest, c))

            def narrow(key, xh, xl):
                wh, wl = weights(slice_no[key])
                out = open_bank(pe, key)
                for c in range(KC):
                    ins = parts3(out[:, :], wh[:, c, :], wl[:, c, :], xh[:, c, :], xl[:, c, :], c == 0, c == KC - 1)
                ins.then_inc(results, 1)

            def transposes(key, pieces):
                out = open_bank(pe, key)
                at_ = 0
                for src, n in pieces:
                    ins = pe.transpose(out[0:src.shape[-1], at_:at_ + n], src, ident)
                    at_ += n
                ins.then_inc(results, 1)

            def normed_turn(r, key, src, then=None):
                pe.wait_ge(normed, r + 1)
                for j in range(KC):
                    out = open_bank(pe, (*key, j))
                    for tt in range(TT):
                        ins = pe.matmul(out[:, tt * P:(tt + 1) * P], src[:, tt, j * P:(j + 1) * P], diag[:, tt, :], start=True, stop=True)
                    ins.then_inc(results, 1)
                    if then:
                        then(j)

            def all_taken(name, n, *rest):
                for j in range(n):
                    until_taken(pe, (name, *rest, j))

            def attention(n_items, S, PT, O, scores, p_buf, pT_buf, v_of, width):
                for i in range(n_items + LAG + 1):
                    k = i - LAG
                    if 0 <= k < n_items:
                        until_taken(pe, (S, k))
                        transposes((PT, k), [(p_buf[k % 4][:, b * P:(b + 1) * P], P) for b in range(k % TT + 1)])
                    k = i - LAG - 1
                    if 0 <= k < n_items:
                        out = open_bank(pe, (O, k))
                        until_taken(pe, (PT, k))
                        for b in range(k % TT + 1):
                            ins = pe.matmul(out[:, 0:width], pT_buf[k % 2][:, b, :], v_of(k, b), start=b == 0, stop=b == k % TT)
                        ins.then_inc(results, 1)
                    if i < n_items:
                        scores(i, open_bank(pe, (S, i))).then_inc(results, 1)

            pe.wait_ge(loaded, 48)
            normed_turn(0, ("hT", 0), x_tok)
            for jj in range(4):
                for name in ("cc", "cu", "cb"):
                    feature_major(name, jj, lambda j, name=name: (name, j), hT_hi[0], hT_lo[0],
                                  chunk_taken("hT", 0) if name == "cc" else None)
            for s in range(4):
                feature_major("gconv", s, lambda j: ("gconv", j), hT_hi[0], hT_lo[0])
            narrow(("forget", 0), hT_hi[0], hT_lo[0])
            for s in range(4):
                feature_major("conv_out", s, lambda j: ("conv_out", j), yT_hi, yT_lo, chunk_taken("cb"))
            for name in ("q1", "k1"):
                for s in range(4):
                    feature_major(name, s, lambda j, name=name: (name, j), hT_hi[0], hT_lo[0])
            for s in range(4):
                token_major("v1", s, 256, hT_hi[0], hT_lo[0])
            for s in range(4):
                feature_major("gatt", s, lambda j: ("gatt", j), hT_hi[0], hT_lo[0])
            all_taken("q1", KC)
            all_taken("k1", KC)
            for s in range(4):
                for tp in range(2):
                    until_taken(pe, ("v1", s, tp))
            pe.wait_ge(sem("neg_made"), 1)
            pe.wait_ge(const_made, 5)

            def scores1(i, out):
                h, qt = i // TT, i % TT
                rows, c, n = slice(64 * (h % 2), 64 * (h % 2) + 64), h // 2, (qt + 1) * P
                pe.matmul(out[:, 0:n], q1T[rows, c, qt * P:n], k1T[rows, c, 0:n], start=True, stop=False)
                pick = pick_r[:, h:h + 1].to_broadcast([P, P])
                pe.matmul(out[:, 0:n], pick, neg[:, 0:n], start=False, stop=False)
                return pe.matmul(out[:, qt * P:n], id_b[:, :], causal_b[:, :], start=False, stop=True)

            attention(H1 * TT, "S1", "PT1", "O1", scores1, p_t, pT_t,
                      lambda i, b: v1[:, b, (i // TT) * HD1:(i // TT + 1) * HD1], HD1)
            for i in range(H1 * TT - 8, H1 * TT):
                until_taken(pe, ("O1", i))
            for j in range(KC):
                transposes(("OT1", j), [(o1_tok[:, tt, j * P:(j + 1) * P], P) for tt in range(TT)])
            for s in range(4):
                feature_major("att_out", s, lambda j: ("att_out", j), o1T_hi, o1T_lo, chunk_taken("OT1"))
            for s in range(4):
                token_major("mix_out", s, 256, mixT_hi, mixT_lo, chunk_taken("att_out"))
            pe.wait_ge(router_loaded, 16)

            def logits_of(c):
                until_taken(pe, ("h2T", c))
                out = bank_of(("logits", 0)) if c else open_bank(pe, ("logits", 0))
                for tt in range(TT):
                    ins = pe.matmul(out[:, tt * 36:(tt + 1) * 36], h2T[:, c, tt * P:(tt + 1) * P], w_router[:, c, :],
                                    start=c == 0 and tt == 0, stop=c == KC - 1, skip_group_check=True)
                return ins

            normed_turn(1, ("h2T",), x1_tok, lambda j: logits_of(j - 2) if j >= 2 else None)
            logits_of(KC - 2)
            logits_of(KC - 1).then_inc(results, 1)
            pe.wait_ge(sem("hots_made"), 1)
            out = open_bank(pe, ("ranks", 0))
            for tt in range(TT):
                for b in range(tt + 1):
                    pe.matmul(out[:, tt * NE:(tt + 1) * NE], up_b[:, :] if b == tt else ones_b[:, :],
                              hots[:, b, :, :].rearrange("p g e -> p (g e)"), start=b == 0, stop=b == tt)
            for b in range(TT):
                ins = pe.matmul(out[:, TT * NE:(TT + 1) * NE], ones_b[:, :], hots[:, b, :, :].rearrange("p g e -> p (g e)"),
                                start=b == 0, stop=b == TT - 1)
            ins.then_inc(results, 1)
            pe.wait_ge(sem("slots_made"), 1)
            out = open_bank(pe, ("table", 0))
            for q in range(TOPK * TT):
                ins = pe.matmul(out[0:CAP, 0:NBLK], hot_slot[:, q, :], hot_block[:, q, :], start=q == 0, stop=q == TOPK * TT - 1)
            ins.then_inc(results, 1)
            for b in range(8):
                pe.wait_ge(drained[b], moe_drained(b))

            def turn_rows(p, done):
                for j in range(KC):
                    ins = pe.transpose(bank[p][:, j * CAP:(j + 1) * CAP], xg[p][:, j * P:(j + 1) * P], ident[0:CAP, 0:CAP])
                ins.then_inc(done, 1)

            def up_product(out, w, x, done, out2=None, half_done=None):
                for f in range(FC):
                    to, g = (out2, f - FC // 2) if out2 is not None and f >= FC // 2 else (out, f)
                    for c in range(KC):
                        ins = pe.matmul(to[:, g * CAP:(g + 1) * CAP], w[:, c, f * P:(f + 1) * P], x[:, c, :],
                                        start=c == 0, stop=c == KC - 1)
                    if half_done is not None and f == FC // 2 - 1:
                        ins.then_inc(half_done, 1)
                ins.then_inc(done, 1)

            def down_product(w, x, done):
                for a in range(2):
                    for f in range(FC):
                        ins = pe.matmul(bank[6 + a][0:CAP, :], x[:, f, :], w[:, f, a * 512:(a + 1) * 512],
                                        start=f == 0, stop=f == FC - 1)
                ins.then_inc(done, 1)

            pe.wait_ge(gathered[0], 16)
            turn_rows(0, xt_turned)
            with pe.Fori(0, NE // 2) as i:
                for p in range(2):
                    pe.wait_ge(xt_made, i * 2 + (p + 1))
                    pe.wait_ge(gate_landed[p], i * 16 + 16)
                    up_product(bank[2 + p], ring_gate[p], xT[p], gate_made)
                    pe.wait_ge(up_landed[p], i * 16 + 16)
                    up_product(bank[4 + p], ring_up[p], xT[p], up_made, bank[p], up_half)
                    pe.wait_ge(gathered[1 - p], i * 16 + 16 * (1 + p))
                    pe.sem_inc(turn, 1)
                    turn_rows(1 - p, xt_turned)
                    pe.wait_ge(down_lo_made, i * 2 + (p + 1))
                    pe.wait_ge(y_taken, i * 2 + (p + 1))
                    for f in range(FC):
                        if f == 0:
                            pe.wait_ge(hx_half, i * 2 + (p + 1))
                        if f == FC // 2:
                            pe.wait_ge(hx_made, i * 2 + (p + 1))
                        for a in range(2):
                            half = slice(a * 512, (a + 1) * 512)
                            ins = parts3(bank[6 + a][:, :], hx_hi[p][:, f, :], hx_lo[p][:, f, :], down_hi[:, f, half],
                                         down_lo[p][:, f, half], f == 0, f == FC - 1)
                    ins.then_inc(y_made, 1)
            count, _ = over_values(pe)
            with pe.If(count > 0):
                with pe.Fori(0, OVF) as i:
                    with pe.If(count > i):
                        pe.wait_ge(sem("ovf_x"), i * 16 + 16)
                        pe.sem_inc(turn, 1)
                        turn_rows(0, sem("ovf_turned"))
                        pe.wait_ge(sem("ovf_xt"), i + 1)
                        pe.wait_ge(sem("ovf_gate"), i * 16 + 16)
                        up_product(bank[2], ring_gate[0], xT[0], sem("ovf_gate_made"))
                        pe.wait_ge(sem("ovf_up"), i * 16 + 16)
                        up_product(bank[4], ring_up[0], xT[0], sem("ovf_up_made"))
                        pe.wait_ge(sem("ovf_hx"), i + 1)
                        pe.wait_ge(sem("ovf_down"), i * 16 + 16)
                        down_product(ring_down[0], hx[0], sem("ovf_y_made"))
            pe.wait_ge(moe_done, 1)
            normed_turn(2, ("hT", 1), x2g_tok)
            for s in range(4):
                feature_major("xm", s, lambda j: ("xm", j), hT_hi[1], hT_lo[1], chunk_taken("hT", 1))
            narrow(("gates", 0), hT_hi[1], hT_lo[1])
            for s in range(4):
                token_major("om", s, 256, hT_hi[1], hT_lo[1])
            all_taken("xm", KC)
            wh, wl = weights(slice_no[("v2", 0)])
            for h in range(MH):
                for tp in range(2):
                    out = open_bank(pe, ("v2", h, tp))
                    for a in range(2):
                        tk = slice((2 * tp + a) * P, (2 * tp + a + 1) * P)
                        for c in (2 * h, 2 * h + 1):
                            ins = parts3(out[:, a * MD:(a + 1) * MD], xmT_hi[:, c, tk], xmT_lo[:, c, tk], wh[:, c, :], wl[:, c, :],
                                         c == 2 * h, c == 2 * h + 1)
                    ins.then_inc(results, 1)
            pe.wait_ge(sem("xc_lo"), KC)
            pe.wait_ge(sem("xc_hi"), KC)
            for name in ("q2", "k2"):
                wh, wl = weights(slice_no[(name, 0)])
                for j in range(KC):
                    h, a = j // 2, j % 2
                    out = open_bank(pe, (name, j))
                    for c in (2 * h, 2 * h + 1):
                        ins = parts3(out[:, :], wh[:, c, a * P:(a + 1) * P], wl[:, c, a * P:(a + 1) * P], xcT_hi[:, c, :],
                                     xcT_lo[:, c, :], c == 2 * h, c == 2 * h + 1)
                    ins.then_inc(results, 1)
            pe.wait_ge(sem("g_em_made"), 1)
            out = open_bank(pe, ("cols", 0))
            for k, src in enumerate((g_i, g_e)):
                for tt in range(TT):
                    ins = pe.transpose(out[:, (k * TT + tt) * MH:(k * TT + tt + 1) * MH], src[:, tt * P:(tt + 1) * P],
                                       ident[0:MH, 0:MH])
            ins.then_inc(results, 1)
            all_taken("q2", KC)
            all_taken("k2", KC)
            pe.wait_ge(sem("nm_made"), 1)
            starts = [0, 512, 896, 1152]
            for h in range(MH + 1):
                if h < MH:
                    out = open_bank(pe, ("mrow", h))
                    pick = pick_r[:, h:h + 1].to_broadcast([P, P])
                    pe.matmul(out[:, :], pick, neg_m[:, :], start=True, stop=True).then_inc(results, 1)
                    for sb in range(TT):
                        out = open_bank(pe, ("ST", h, sb))
                        n = (TT - sb) * P
                        for c in (2 * h, 2 * h + 1):
                            ins = pe.matmul(out[:, 0:n], k2T[:, c, sb * P:(sb + 1) * P], q2T[:, c, sb * P:SEQ],
                                            start=c == 2 * h, stop=c == 2 * h + 1)
                        ins.then_inc(results, 1)
                if h >= 1:
                    g = h - 1
                    for tt in range(TT):
                        if tt == 0:
                            for hh in range(MH):
                                for tp in range(2):
                                    until_taken(pe, ("v2", hh, tp))
                        out = open_bank(pe, ("num", g, tt))
                        for sb in range(tt + 1):
                            until_taken(pe, ("ST", g, sb))
                            w = sw[g % 2][:, starts[sb] + (tt - sb) * P:starts[sb] + (tt - sb + 1) * P]
                            pe.matmul(out[:, 0:MD], w, v2[:, sb, g, :], start=sb == 0, stop=sb == tt, skip_group_check=True)
                            ins = pe.matmul(out[:, MD:MD + 2], w, const[:, C_ONE:C_ONE + 2], start=False, stop=sb == tt,
                                            skip_group_check=True)
                        ins.then_inc(results, 1)
            for s in range(4):
                feature_major("zm", s, lambda j: ("zm", j), hT_hi[1], hT_lo[1])
            pe.wait_ge(sem("head_normed"), MH * TT)
            for j in range(KC):
                transposes(("hmT", j), [(hm_tok[:, tt, j // 2, (j % 2) * P:(j % 2 + 1) * P], P) for tt in range(TT)])
            for s in range(4):
                feature_major("xp", s, lambda j: ("xp", j), hT_hi[1], hT_lo[1])
            for s in range(4):
                feature_major("zp", s, lambda j: ("zp", j), hT_hi[1], hT_lo[1])
            pe.wait_ge(sem("mean_made"), KC)
            wh, wl = weights(slice_no[("pool", 0)])
            for j in range(KC):
                g, a = j // 2, j % 2
                out = open_bank(pe, ("pool", j))
                for c in (2 * g, 2 * g + 1):
                    ins = parts3(out[:, :], wh[:, c, a * P:(a + 1) * P], wl[:, c, a * P:(a + 1) * P], poolT_hi[:, c, :],
                                 poolT_lo[:, c, :], c == 2 * g, c == 2 * g + 1)
                ins.then_inc(results, 1)
            pe.wait_ge(sem("ya_lo_made"), KC)
            for c4 in range(4):
                banks = [open_bank(pe, ("w_out2", c4, tt)) for tt in range(TT)]
                for b, (xh, xl) in enumerate(((ya_hi, ya_lo), (yb_hi, yb_lo))):
                    if c4 == 0 and b == 1:
                        all_taken("pool", KC)
                    wh, wl = weights(slice_no[("w_out2", c4, b)])
                    for tt in range(TT):
                        tk = slice(tt * P, (tt + 1) * P)
                        for c in range(KC):
                            ins = parts3(banks[tt][:, 0:256], xh[:, c, tk], xl[:, c, tk], wh[:, c, :], wl[:, c, :],
                                         b == 0 and c == 0, b == 1 and c == KC - 1)
                        if b == 1:
                            ins.then_inc(results, 1)
                        elif tt == TT - 1:
                            ins.then_inc(sem("half_used"), 1)
            normed_turn(3, ("hT", 2), x4_tok)
            for s, n in enumerate((256, 256, 192)):
                token_major("cin", s, n, hT_hi[2], hT_lo[2], chunk_taken("hT", 2))
            for s in range(4):
                feature_major("z3", s, lambda j: ("z3", j), hT_hi[2], hT_lo[2])
            pe.wait_ge(sem("c_normed"), 2 * TT)
            for j in range(5):
                transposes(("cT", j), [(c_tok[:, tt, j * P:(j + 1) * P], P) for tt in range(TT)])
            all_taken("cT", 5)
            nq = QL // P

            def turn_q(s):
                for tt in range(TT):
                    until_taken(pe, ("uq", s, tt))
                for a in range(2):
                    transposes(("qnT", s, a), [(qb[:, tt, a, 0:NOPE], P) for tt in range(TT)])
                pe.wait_ge(sem("q_roped"), s + 1)
                transposes(("qpT", s), [(qr[:, tt, :, :].rearrange("p h n -> p (h n)"), P) for tt in range(TT)])

            def turn_k(s):
                pe.wait_ge(sem("k_normed"), s + 1)
                for a in range(2):
                    transposes(("knT", s, a), [(kb[:, tt, a, :], P) for tt in range(TT)])
                transposes(("kpT", s), [(kr[:, tt, :, :].rearrange("p h n -> p (h n)"), P) for tt in range(TT)])

            for s in range(4):
                for name, c0, c1, n in (("uq", 0, nq, 2 * QKH), ("ukv", nq, 5, 512)):
                    wh, wl = weights(slice_no[(name, s)])
                    for tt in range(TT):
                        out = open_bank(pe, (name, s, tt))
                        tk = slice(tt * P, (tt + 1) * P)
                        for c in range(c0, c1):
                            ins = parts3(out[:, 0:n], cT_hi[:, c, tk], cT_lo[:, c, tk], wh[:, c - c0, :], wl[:, c - c0, :],
                                         c == c0, c == c1 - 1)
                        ins.then_inc(results, 1)
                    if name == "uq" and s >= 1:
                        turn_k(s - 1)
                turn_q(s)
            turn_k(3)
            for s in range(4):
                for a in range(2):
                    until_taken(pe, ("qnT", s, a))
                    until_taken(pe, ("knT", s, a))
                until_taken(pe, ("qpT", s))
                until_taken(pe, ("kpT", s))
                for tt in range(TT):
                    until_taken(pe, ("ukv", s, tt))

            def scores3(i, out):
                h, qt = i // TT, i % TT
                rows, c, n = slice(64 * (h % 2), 64 * (h % 2) + 64), h // 2, (qt + 1) * P
                pe.matmul(out[:, 0:n], qnT[:, h, qt * P:n], knT[:, h, 0:n], start=True, stop=False)
                pe.matmul(out[:, 0:n], qpT[rows, c, qt * P:n], kpT[rows, c, 0:n], start=False, stop=False)
                return pe.matmul(out[:, qt * P:n], id_b[:, :], block_b[:, :], start=False, stop=True)

            attention(CH * TT, "S3", "PT3", "O3", scores3, p3_t, pT3_t, lambda i, b: v3[:, b, i // TT, :], VH)
            for i in range(CH * TT - 8, CH * TT):
                until_taken(pe, ("O3", i))
            for j in range(KC):
                transposes(("OT3", j), [(o3_tok[:, tt, j * P:(j + 1) * P], P) for tt in range(TT)])
            for s in range(4):
                token_major("out3", s, 256, yT3_hi, yT3_lo, lambda c: pe.wait_ge(sem("y3_lo_made"), c + 1))

        @block.vector
        def _(dve):
            steps, his, ssqs, norms = [0], [0], [0], [0]
            V = nc.vector

            def step(ins):
                steps[0] += 1
                ins.then_inc(dve_step, 1)
                dve.wait_ge(dve_step, steps[0])

            def split(n, end):
                if n >= end:
                    return
                dve.wait_ge(w_landed[n % RINGS], 16 * (n // RINGS + 1))
                dve.wait_ge(w_hi_made, n + 1)
                V.tensor_tensor(ring_view(w_lo, n), ring_view(raw, n), ring_view(w_hi, n).bitcast(F32), ALU.subtract)\
                    .then_inc(w_lo_made, 1)

            def evict_lo(key, hi, lo, scale=None):
                src = until_made(dve, key)
                his[0] += 1
                dve.wait_ge(hi_made, his[0])
                took(V.scalar_tensor_tensor(out=lo, in0=src[:, :], scalar=1.0 if scale is None else scale,
                                            in1=hi.bitcast(F32), op0=ALU.mult, op1=ALU.subtract), key)

            def rsqrt(n, width, waits, src=ssq, quarters=False):
                ssqs[0] += waits
                if waits:
                    dve.wait_ge(ssq_made, ssqs[0])
                if quarters:
                    step(V.tensor_reduce(ssum[:, 0:TT], ssq[:, :].rearrange("p (t s) -> p t s", s=4), AX_X, ALU.add))
                    src = ssum
                norms[0] += 1
                if isinstance(width, tuple):
                    for a, b, w in width:
                        ins = V.tensor_scalar(var[:, a:b], src[:, a:b], 1.0 / w, EPS, ALU.mult, ALU.add)
                else:
                    ins = V.tensor_scalar(var[:, 0:n], src[:, 0:n], 1.0 / width, EPS, ALU.mult, ALU.add)
                ins.then_inc(var_made, 1)
                dve.wait_ge(var_made, norms[0])
                dve.wait_ge(root_made, norms[0])
                r, w, v = rstd[:, 0:n], newton[:, 0:n], var[:, 0:n]
                step(V.reciprocal(r, root[:, 0:n]))
                step(V.tensor_tensor(w, r, r, ALU.mult))
                step(V.tensor_tensor(w, w, v, ALU.mult))
                step(V.tensor_scalar(w, w, -0.5, 1.5, ALU.mult, ALU.add))
                step(V.tensor_tensor(r, r, w, ALU.mult))

            def diagonals(by=None):
                if by is not None:
                    step(V.tensor_tensor(rstd[:, 0:TT], rstd[:, 0:TT], by, ALU.mult))
                V.tensor_tensor(diag[:, :, :], ident.unsqueeze(1).to_broadcast([P, TT, P]),
                                rstd[:, 0:TT].unsqueeze(2).to_broadcast([P, TT, P]), ALU.mult).then_inc(normed, 1)

            def split_sum(val, hi, lo):
                step(V.tensor_copy(hi, val))
                return V.tensor_tensor(lo, val, hi.bitcast(F32), ALU.subtract)

            rsqrt(TT, D, TT)
            dve.wait_ge(loaded, 48)
            diagonals()
            split(0, slices1)
            for j in range(KC):
                evict_lo(("hT", 0, j), hT_hi[0][:, j, :], hT_lo[0][:, j, :], vcol("norm_mix_g", j))
            split(1, slices1)
            for jj in range(4):
                n = slice_no[("cc", jj)]
                split(n + 2, slices1)
                for j in (2 * jj, 2 * jj + 1):
                    z, acc = z_t[j % 2], acc_t[j % 2]
                    src = until_made(dve, ("cu", j))
                    until_taken(dve, ("cc", j))
                    V.tensor_tensor(z[:, :], src[:, :], cc_t[j % 2][:, :], ALU.mult).then_inc(z_made, 1)
                    dve.wait_ge(z_made, j + 1)
                    step(V.tensor_scalar(acc[:, :], z[:, :], vcol("conv_w2", j), vcol("conv_b", j), ALU.mult, ALU.add))
                    step(V.scalar_tensor_tensor(out=acc[:, 1:], in0=z[:, 0:SEQ - 1], scalar=vcol("conv_w1", j), in1=acc[:, 1:],
                                                op0=ALU.mult, op1=ALU.add))
                    took(V.scalar_tensor_tensor(out=acc[:, 2:], in0=z[:, 0:SEQ - 2], scalar=vcol("conv_w0", j), in1=acc[:, 2:],
                                                op0=ALU.mult, op1=ALU.add), ("cu", j))
                    until_taken(dve, ("cu", j))
                split(n + 3, slices1)
                for j in (2 * jj, 2 * jj + 1):
                    acc = acc_t[j % 2]
                    src = until_made(dve, ("cb", j))
                    step(V.tensor_tensor(acc[:, :], src[:, :], acc[:, :], ALU.mult))
                    took(split_sum(acc[:, :], yT_hi[:, j, :], yT_lo[:, j, :]), ("cb", j))
                split(n + 4, slices1)
            for s in range(4):
                until_made(dve, ("gconv", 2 * s + 1))
                split(slice_no[("gconv", s)] + 2, slices1)
            def log_gate(src, x, ab, logs, one, bias, made, log_made):
                step(V.tensor_scalar(x[:, :], src, bias, None, ALU.add))
                V.scalar_tensor_tensor(out=ab[:, :], in0=x[:, :], scalar=-1.0, in1=x[:, :], op0=ALU.mult, op1=ALU.max)\
                    .then_inc(made, 1)
                dve.wait_ge(log_made, 1)
                step(V.scalar_tensor_tensor(out=ab[:, :], in0=x[:, :], scalar=0.0, in1=logs[:, :], op0=ALU.min, op1=ALU.subtract))
                step(V.tensor_tensor_scan(x[:, :], one[:, :], ab[:, :], 0.0, ALU.mult, ALU.add))

            def conv_gate(j):
                src = until_made(dve, ("conv_out", j))
                until_taken(dve, ("gconv", j))
                took(V.tensor_tensor(mixT[:, j, :], src[:, :], mixT[:, j, :], ALU.mult), ("conv_out", j))

            until_made(dve, ("forget", 0))
            split(slice_no[("forget", 0)] + 2, slices1)
            step(V.memset(neg[:, :].bitcast(F32), 0.0))
            step(V.memset(f_one[:, :], 1.0))
            step(V.tensor_tensor(pick_r[:, :], ident[:, 0:H1], ident[:, LO:LO + H1], ALU.add))
            for s in range(4):
                if s == 1:
                    src = until_made(dve, ("forget", 0))
                    log_gate(src[0:H1, :], f_x, f_abs, f_l, f_one, vec[0:H1, V_BF:V_BF + 1], sem("f_abs_made"), sem("f_log_made"))
                    step(V.tensor_scalar(f_abs[:, :], f_x[:, :], -1.0, None, ALU.mult))
                    step(V.tensor_copy(neg[0:H1, :], f_abs[:, :]))
                    took(V.tensor_tensor(neg[LO:LO + H1, :], f_abs[:, :], neg[0:H1, :].bitcast(F32), ALU.subtract), ("forget", 0))
                conv_gate(2 * s)
                conv_gate(2 * s + 1)
                split(slice_no[("conv_out", s)] + 2, slices1)
            until_taken(dve, ("forget", 0))
            V.memset(mark[:, 1:2], 1.0).then_inc(sem("neg_made"), 1)
            for name in ("q1", "k1"):
                for s in range(4):
                    until_made(dve, (name, 2 * s + 1))
                    split(slice_no[(name, s)] + 2, slices1)
            for s in range(4):
                until_made(dve, ("v1", s, 1))
                split(slice_no[("v1", s)] + 2, slices1)
            for s in range(4):
                until_made(dve, ("gatt", 2 * s + 1))
                split(slice_no[("gatt", s)] + 2, slices1)

            def attention(n_items, S, PT, O, max_of, pT_buf, o_of, width):
                for i in range(n_items + LAG + 1):
                    k = i - LAG
                    if 0 <= k < n_items and k % 2 == 1:
                        keys = (k % TT + 1) * P
                        src = until_made(dve, (PT, k))
                        if k >= 2:
                            dve.wait_ge(results, order[(O, k - 2)] + 1)
                        took(V.tensor_copy(pT_buf[k % 2][:, 0:k % TT + 1, :], src[:, 0:keys].rearrange("p (k q) -> p k q", q=P)), (PT, k))
                    k = i - LAG - 1
                    if 0 <= k < n_items:
                        src = until_made(dve, (O, k))
                        until_taken(dve, (S, k))
                        step(V.reciprocal(inv_sum[:, k % 8:k % 8 + 1], row_sum[:, k % 8:k % 8 + 1]))
                        took(V.tensor_scalar(o_of(k), src[:, 0:width], inv_sum[:, k % 8:k % 8 + 1], None, ALU.mult), (O, k))
                    if i < n_items:
                        keys = (i % TT + 1) * P
                        src = until_made(dve, (S, i))
                        if i >= 8:
                            until_taken(dve, (S, i - 8))
                        max_of(i, src[:, 0:keys])

            def max1(i, src):
                V.tensor_reduce(neg_max[:, i % 8:i % 8 + 1], src, AX_X, ALU.max, negate=True).then_inc(sem("max1_made"), 1)

            attention(H1 * TT, "S1", "PT1", "O1", max1, pT_t, lambda k: o1_tok[:, k % TT, (k // TT) * HD1:(k // TT + 1) * HD1], HD1)
            for j in range(KC):
                evict_lo(("OT1", j), o1T_hi[:, j, :], o1T_lo[:, j, :])
            for s in range(4):
                for j in (2 * s, 2 * s + 1):
                    acc = acc_t[j % 2]
                    src = until_made(dve, ("att_out", j))
                    until_taken(dve, ("gatt", j))
                    step(V.tensor_tensor(acc[:, :], src[:, :], gattT[:, j, :], ALU.mult))
                    step(V.tensor_tensor(acc[:, :], acc[:, :], mixT[:, j, :], ALU.add))
                    took(split_sum(acc[:, :], mixT_hi[:, j, :], mixT_lo[:, j, :]), ("att_out", j))
                split(slice_no[("att_out", s)] + 2, slices1)
            dve.wait_ge(x_back, 16)
            for s in range(4):
                for tp in range(2):
                    src = until_made(dve, ("mix_out", s, tp))
                    xv = x1_tok[:, 2 * tp:2 * tp + 2, 256 * s:256 * s + 256]
                    took(V.tensor_tensor(xv, src[:, :].rearrange("p (t n) -> p t n", t=2), xv, ALU.add), ("mix_out", s, tp))
                split(slice_no[("mix_out", s)] + 2, slices1)
            rsqrt(TT, D, 4 * TT, quarters=True)
            diagonals()
            src = until_made(dve, ("logits", 0))
            took(V.tensor_copy(lg[:, :, :], src[:, 0:TT * 36].rearrange("p (t n) -> p t n", t=TT)), ("logits", 0))
            until_taken(dve, ("logits", 0))
            lg_g = lg[:, :, 0:NG]
            lg_e = lg[:, :, NG:].rearrange("p t (g e) -> p t g e", g=NG)
            iota, back = const[:, C_IOTA:C_IOTA + CAP], const[:, C_BACK:C_BACK + EPG]
            over_t = lambda a, n: a.unsqueeze(1).to_broadcast([P, TT, n])
            on_row = lambda a, n: a.unsqueeze(2).to_broadcast([P, TT, n])
            on_q = lambda a, n: a.unsqueeze(2).to_broadcast([P, TOPK * TT, n])
            over_q = lambda a, n: a.unsqueeze(1).to_broadcast([P, TOPK * TT, n])

            def first_of(vals, top, n, cand_, one, low):
                step(V.tensor_tensor(one, vals, on_row(top, n), ALU.is_ge))
                step(V.tensor_tensor(cand_, over_t(back[:, 0:n], n), one, ALU.mult))
                step(V.tensor_reduce(low, cand_, AX_X, ALU.min))
                step(V.tensor_tensor(one, over_t(back[:, 0:n], n), on_row(low, n), ALU.is_equal))

            g_top, low, g_val, top1, top2, dif, e2, den = (sm[:, k, 0:4] for k in range(8))
            step(V.tensor_reduce(g_top, lg_g, AX_X, ALU.max))
            first_of(lg_g, g_top, NG, cand_g[:, :, :], one_g[:, :, :], low)
            V.tensor_tensor(cand_g[:, :, :], lg_g, on_row(g_top, NG), ALU.subtract).then_inc(sem("router_e1"), 1)
            step(V.tensor_tensor(wide[:, :, :, :], lg_e, one_g[:, :, :].unsqueeze(3).to_broadcast([P, TT, NG, EPG]), ALU.mult))
            step(V.tensor_reduce(les[:, :, :], wide[:, :, :, :].rearrange("p t g e -> p t e g"), AX_X, ALU.add))
            step(V.tensor_reduce(top1, les[:, :, :], AX_X, ALU.max))
            first_of(les[:, :, :], top1, EPG, cand[:, :, :], one1[:, :, :], low)
            step(V.scalar_tensor_tensor(out=les2[:, :, :], in0=one1[:, :, :], scalar=MASKED, in1=les[:, :, :],
                                        op0=ALU.mult, op1=ALU.add))
            step(V.tensor_reduce(top2, les2[:, :, :], AX_X, ALU.max))
            first_of(les2[:, :, :], top2, EPG, cand[:, :, :], one2[:, :, :], low)
            for k, one in enumerate((one1, one2)):
                ins = V.tensor_tensor(hot[:, k, :, :, :], one[:, :, :].unsqueeze(2).to_broadcast([P, TT, NG, EPG]),
                                      one_g[:, :, :].unsqueeze(3).to_broadcast([P, TT, NG, EPG]), ALU.mult)
            step(ins)
            V.tensor_tensor(hots[:, :, :, :], hot[:, 0, :, :, :], hot[:, 1, :, :, :], ALU.add).then_inc(sem("hots_made"), 1)
            V.tensor_tensor(dif, top2, top1, ALU.subtract).then_inc(sem("router_e3"), 1)
            dve.wait_ge(sem("router_e2"), 1)
            step(V.memset(ones_e[:, :], 1.0))
            step(V.tensor_reduce(g_val, eg[:, :, :], AX_X, ALU.add))
            step(V.reciprocal(g_val, g_val))
            src = until_made(dve, ("ranks", 0))
            of_expert = hot[:, :, :, :, :].rearrange("p k t g e -> p k t (g e)")
            wide2 = hot_slot[:, :, 0:NE].rearrange("p (k t) e -> p k t e", k=TOPK)
            V.tensor_scalar(counts[:, 8:], src[:, TT * NE:(TT + 1) * NE], -1.0, None, ALU.add)
            step(V.tensor_tensor(wide2, of_expert, src[:, 0:TT * NE].rearrange("p (t e) -> p t e", t=TT).unsqueeze(1)
                                 .to_broadcast([P, TOPK, TT, NE]), ALU.mult))
            step(V.tensor_reduce(counts[:, 0:8], hot_slot[:, :, 0:NE], AX_X, ALU.add))
            step(V.tensor_scalar(blocks[:, :], counts[:, :], 1.0 / CAP, 0.5 / CAP - 0.5, ALU.mult, ALU.add))
            step(V.tensor_scalar(blocks[:, :], blocks[:, :], ROUNDER, None, ALU.add))
            took(V.tensor_scalar(blocks[:, :], blocks[:, :], -ROUNDER, None, ALU.add), ("ranks", 0))
            until_taken(dve, ("ranks", 0))
            step(V.tensor_scalar(novf[:, :], blocks[:, 8:], 0.0, None, ALU.max))
            step(V.tensor_tensor_scan(incl[:, :], ones_e[:, :], novf[:, :], 0.0, ALU.mult, ALU.add))
            step(V.tensor_tensor(first[:, :], incl[:, :], novf[:, :], ALU.subtract))
            step(V.tensor_tensor(wide2, of_expert, first[:, :].unsqueeze(1).unsqueeze(1).to_broadcast([P, TOPK, TT, NE]), ALU.mult))
            start, slot, low_row, high_row = (sm[:, k, :] for k in range(10, 14))
            row = const[:, C_ROW:C_SPARE]
            V.tensor_reduce(start, hot_slot[:, :, 0:NE], AX_X, ALU.add)
            V.scalar_tensor_tensor(out=slot, in0=blocks[:, 0:8], scalar=-float(CAP), in1=counts[:, 0:8], op0=ALU.mult, op1=ALU.add)
            step(V.scalar_tensor_tensor(out=low_row, in0=blocks[:, 0:8], scalar=0.5, in1=row, op0=ALU.is_lt, op1=ALU.mult))
            V.tensor_tensor(high_row, row, low_row, ALU.subtract)
            step(V.tensor_tensor(start, start, blocks[:, 0:8], ALU.add))
            V.tensor_tensor(hot_slot[:, :, :], over_q(iota, CAP), on_q(slot, CAP), ALU.is_equal)
            V.tensor_tensor(hot_block[:, :, 0:NE], of_expert.rearrange("p k t e -> p (k t) e"), on_q(low_row, NE), ALU.mult)
            step(V.tensor_tensor(hot_block[:, :, NE:], over_q(iota[:, 1:17], 16), on_q(start, 16), ALU.is_equal))
            V.tensor_tensor(hot_block[:, :, NE:], hot_block[:, :, NE:], on_q(high_row, 16), ALU.mult).then_inc(sem("slots_made"), 1)
            src = until_made(dve, ("table", 0))
            took(V.tensor_scalar(slot_r[:, :], src[0:CAP, 0:NBLK], -1.0, None, ALU.add), ("table", 0))
            until_taken(dve, ("table", 0))
            V.tensor_scalar(slot_u[:, :], slot_r[:, :], 0.0, None, ALU.is_lt)
            step(V.tensor_scalar(slot_g[:, :], slot_r[:, :], float(SEQ), None, ALU.is_ge))
            V.scalar_tensor_tensor(out=slot_u[:, :], in0=slot_u[:, :], scalar=const[0:CAP, C_SPARE:C_SPARE + 1], in1=slot_r[:, :],
                                   op0=ALU.mult, op1=ALU.add)
            step(V.scalar_tensor_tensor(out=slot_g[:, :], in0=slot_g[:, :], scalar=-float(SEQ), in1=slot_r[:, :], op0=ALU.mult, op1=ALU.add))
            step(V.tensor_scalar(slot_g[:, :], slot_g[:, :], 0.0, None, ALU.max))
            V.tensor_copy(table[:, :, 1], slot_u[:, :])
            V.tensor_copy(table[:, :, 0], slot_g[:, :]).then_inc(sem("table_made"), 1)
            step(V.tensor_tensor(ovt[:, :, :], incl[:, :].unsqueeze(1).to_broadcast([P, 16, NE]),
                                 iota[:, 0:16].unsqueeze(2).to_broadcast([P, 16, NE]), ALU.is_le))
            step(V.tensor_reduce(ovs[:, 0:16], ovt[:, :, :], AX_X, ALU.add))
            step(V.tensor_scalar(ovs[:, 0:16], ovs[:, 0:16], float(NE - 1), None, ALU.min))
            step(V.tensor_copy(ovs[:, 16:17], incl[:, NE - 1:NE]))
            V.tensor_copy(over[:, 0:17], ovs[:, 0:17]).then_inc(sem("over_made"), 1)
            dve.wait_ge(sem("router_e4"), 1)
            step(V.tensor_scalar(den, e2, 1.0, None, ALU.add))
            step(V.reciprocal(den, den))
            step(V.tensor_tensor(tok_w[:, 0, :], den, g_val, ALU.mult))
            step(V.tensor_tensor(tok_w[:, 1, :], tok_w[:, 0, :], e2, ALU.mult))
            gain = vec[:, VECS.index("norm_ffn_g") * KC:(VECS.index("norm_ffn_g") + 1) * KC].unsqueeze(2).to_broadcast([P, KC, CAP])

            def rows_in(p, done):
                V.tensor_tensor(xT[p][:, :, :], bank[p][:, :].rearrange("p (c n) -> p c n", c=KC), gain, ALU.mult).then_inc(done, 1)

            def gated(p, b, done):
                V.tensor_tensor(hx[p][:, :, :], sg[p][:, :, :], bank[b][:, 0:FC * CAP].rearrange("p (f c) -> p f c", f=FC),
                                ALU.mult).then_inc(done, 1)

            dve.wait_ge(results, order[("logits", 0)] + 1)
            for p in range(2):
                V.memset(hx_hi[p][:, :, :].bitcast(F32), 0.0)
                step(V.memset(hx_lo[p][:, :, :].bitcast(F32), 0.0))
            dve.wait_ge(xt_turned, 1)
            rows_in(0, xt_made)
            with dve.Fori(0, NE // 2) as i:
                for p in range(2):
                    dve.wait_ge(down_landed[p], i * 16 + 16)
                    dve.wait_ge(down_hi_made, i * 2 + (p + 1))
                    V.tensor_tensor(down_lo[p][:, :, :], ring_down[p][:, :, :], down_hi[:, :, :].bitcast(F32), ALU.subtract)\
                        .then_inc(down_lo_made, 1)
                    dve.wait_ge(silu_made, i * 2 + (p + 1))
                    for half in range(2):
                        n = FC // 2
                        fs, k = slice(half * n, half * n + n), 2 * p + half + 1
                        dve.wait_ge((up_half, up_made)[half], i * 2 + (p + 1))
                        V.tensor_tensor(hx[p][:, fs, :], sg[p][:, fs, :],
                                        bank[(4 + p, p)[half]][:, 0:n * CAP].rearrange("p (f c) -> p f c", f=n),
                                        ALU.mult).then_inc(gated_made, 1)
                        dve.wait_ge(gated_made, i * 4 + k)
                        V.tensor_copy(hx_hi[p][:, fs, 0:CAP], hx[p][:, fs, :]).then_inc(hx_hi_made, 1)
                        dve.wait_ge(hx_hi_made, i * 4 + k)
                        V.tensor_tensor(hx_lo[p][:, fs, 0:CAP], hx[p][:, fs, :], hx_hi[p][:, fs, 0:CAP].bitcast(F32), ALU.subtract)\
                            .then_inc((hx_half, hx_made)[half], 1)
                    dve.wait_ge(xt_turned, i * 2 + (p + 2))
                    rows_in(1 - p, xt_made)
            count, _ = over_values(dve)
            with dve.If(count > 0):
                with dve.Fori(0, OVF) as i:
                    with dve.If(count > i):
                        dve.wait_ge(sem("ovf_turned"), i + 1)
                        rows_in(0, sem("ovf_xt"))
                        dve.wait_ge(sem("ovf_silu"), i + 1)
                        dve.wait_ge(sem("ovf_up_made"), i + 1)
                        gated(0, 4, sem("ovf_hx"))
            dve.wait_ge(moe_done, 1)
            for tt in range(TT):
                dve.wait_ge(sem(f"y_loaded{tt}"), 32)
                step(V.scalar_tensor_tensor(out=x1_tok[:, tt, :], in0=y1_tok[:, tt, :], scalar=tok_w[:, 0, tt:tt + 1],
                                            in1=x1_tok[:, tt, :], op0=ALU.mult, op1=ALU.add))
                V.scalar_tensor_tensor(out=x1_tok[:, tt, :], in0=y2_tok[:, tt, :], scalar=tok_w[:, 1, tt:tt + 1],
                                       in1=x1_tok[:, tt, :], op0=ALU.mult, op1=ALU.add).then_inc(sem("x2_made"), 1)
                if tt == 0:
                    dve.wait_ge(gfin_loaded, 16)
                dve.wait_ge(sem("x2_made"), 2 * tt + 1)
                V.tensor_tensor(x2g_tok[:, tt, :], x1_tok[:, tt, :], gfin[:, :], ALU.mult).then_inc(sem("x2_made"), 1)
            split(slices1, n_slices)
            rsqrt(TT, D, 2 * TT)
            step(V.tensor_copy(r_fin[:, :], rstd[:, 0:TT]))
            step(V.tensor_tensor(ssum[:, 0:TT], ssq[:, TT:2 * TT], r_fin[:, :], ALU.mult))
            step(V.tensor_tensor(ssum[:, 0:TT], ssum[:, 0:TT], r_fin[:, :], ALU.mult))
            rsqrt(TT, D, 0, ssum)
            diagonals(r_fin[:, :])
            V.memset(mark[:, 2:3], 0.0).then_inc(sem("r_fin_made"), 1)
            for j in range(KC):
                evict_lo(("hT", 1, j), hT_hi[1][:, j, :], hT_lo[1][:, j, :], vcol("a_norm_g", j))
            split(slices1 + 1, n_slices)
            for s in range(4):
                for j in (2 * s, 2 * s + 1):
                    src = until_made(dve, ("xm", j))
                    his[0] += 1
                    dve.wait_ge(hi_made, his[0])
                    V.tensor_tensor(xmT_lo[:, j, :], src[:, :], xmT_hi[:, j, :].bitcast(F32), ALU.subtract)
                    if j >= 2:
                        dve.wait_ge(sem("xc_hi"), j - 1)
                    cv = cv_t[j % 2]
                    step(V.tensor_scalar(cv[:, :], src[:, :], vcol("a_conv_w3", j), vcol("a_conv_b", j), ALU.mult, ALU.add))
                    for back in (1, 2, 3):
                        ins = V.scalar_tensor_tensor(out=cv[:, back:], in0=src[:, 0:SEQ - back], scalar=vcol(f"a_conv_w{3 - back}", j),
                                                     in1=cv[:, back:], op0=ALU.mult, op1=ALU.add)
                        if back < 3:
                            step(ins)
                    took(ins, ("xm", j))
                    if j == 2 * s:
                        split(slice_no[("xm", s)] + 2, n_slices)
            src = until_made(dve, ("gates", 0))
            split(slice_no[("gates", 0)] + 2, n_slices)
            dve.wait_ge(sem("xc_hi"), KC)
            step(V.memset(neg_m[:, :].bitcast(F32), 0.0))
            step(V.memset(g_one[:, :], 1.0))
            step(V.tensor_scalar(g_i[:, :], src[0:MH, :], vec[0:MH, V_BI:V_BI + 1], None, ALU.add))
            log_gate(src[LO:LO + MH, :], g_x, g_abs, g_l, g_one, vec[0:MH, V_BG:V_BG + 1], sem("g_abs_made"), sem("g_log_made"))
            step(V.tensor_tensor(g_i[:, :], g_i[:, :], g_x[:, :], ALU.subtract))
            step(V.tensor_tensor_scan(g_m[:, :], g_i[:, :], g_i[:, :], 0.0, ALU.max, ALU.max))
            V.tensor_tensor(g_abs[:, :], g_x[:, :], g_m[:, :], ALU.add).then_inc(sem("g_m_made"), 1)
            step(V.tensor_scalar(g_m[:, :], g_m[:, :], -1.0, None, ALU.mult))
            step(V.tensor_copy(neg_m[0:MH, :], g_m[:, :]))
            took(V.tensor_tensor(neg_m[LO:LO + MH, :], g_m[:, :], neg_m[0:MH, :].bitcast(F32), ALU.subtract), ("gates", 0))
            until_taken(dve, ("gates", 0))
            V.memset(mark[:, 1:2], 0.0).then_inc(sem("nm_made"), 1)
            for s in range(4):
                until_made(dve, ("om", s, 1))
                split(slice_no[("om", s)] + 2, n_slices)
            until_made(dve, ("v2", MH - 1, 1))
            split(slice_no[("v2", 0)] + 2, n_slices)
            for name in ("q2", "k2"):
                until_made(dve, (name, KC - 1))
                split(slice_no[(name, 0)] + 2, n_slices)
            src = until_made(dve, ("cols", 0))
            took(V.tensor_copy(cols[:, :, :, :], src[:, 0:2 * TT * MH].rearrange("p (k t h) -> p k t h", k=2, t=TT)), ("cols", 0))
            until_taken(dve, ("cols", 0))
            causalT = const[:, C_CAUSALT:C_BLOCK].unsqueeze(1).to_broadcast([P, TT, P])
            starts = [0, 512, 896, 1152]
            for h in range(MH + 1):
                if h < MH:
                    src = until_made(dve, ("mrow", h))
                    if h >= 1:
                        dve.wait_ge(sem("wexp_made"), TT * h)
                    V.tensor_tensor(mdiag[:, :, :], src[:, :].rearrange("p (t n) -> p t n", t=TT), causalT, ALU.add)\
                        .then_inc(sem("mdiag_made"), 1)
                    for sb in range(TT):
                        k = h * TT + sb
                        src = until_made(dve, ("ST", h, sb))
                        dve.wait_ge(sem("wexp_made"), k + 1)
                        if h >= 2:
                            dve.wait_ge(results, order[("num", h - 2, TT - 1)] + 1)
                        n = (TT - sb) * P
                        if sb == TT - 1:
                            step(V.tensor_tensor(sw[h % 2][:, starts[sb]:starts[sb] + n], src[:, 0:n], wexp[k % 2][:, 0:n], ALU.mult))
                            took(V.memset(newton[:, 0:1], 0.0), ("ST", h, sb))
                            took(V.memset(newton[:, 1:2], 0.0), ("mrow", h))
                        else:
                            took(V.tensor_tensor(sw[h % 2][:, starts[sb]:starts[sb] + n], src[:, 0:n], wexp[k % 2][:, 0:n], ALU.mult),
                                 ("ST", h, sb))
                if h >= 1:
                    g = h - 1
                    for tt in range(TT):
                        src = until_made(dve, ("num", g, tt))
                        for tp in range(2):
                            until_taken(dve, ("om", g, tp))
                        step(V.tensor_copy(den_t[:, 2:3], src[:, MD:MD + 1]))
                        step(V.scalar_tensor_tensor(out=den_t[:, 0:1], in0=den_t[:, 2:3], scalar=-1.0, in1=den_t[:, 2:3],
                                                    op0=ALU.mult, op1=ALU.max))
                        step(V.tensor_tensor(den_t[:, 0:1], den_t[:, 0:1], cols[:, 1, tt, g:g + 1], ALU.max))
                        step(V.reciprocal(den_t[:, 1:2], den_t[:, 0:1]))
                        took(V.scalar_tensor_tensor(out=hm_tok[:, tt, g, :], in0=src[:, 0:MD], scalar=den_t[:, 1:2],
                                                    in1=hm_tok[:, tt, g, :], op0=ALU.mult, op1=ALU.mult), ("num", g, tt))
            rsqrt(TT * MH, MD, TT * MH)
            for tt in range(TT):
                for h in range(MH):
                    V.tensor_scalar(hm_tok[:, tt, h, :], hm_tok[:, tt, h, :], rstd[:, tt * MH + h:tt * MH + h + 1], None, ALU.mult)\
                        .then_inc(sem("head_normed"), 1)
            for s in range(4):
                until_made(dve, ("zm", 2 * s + 1))
                split(slice_no[("zm", s)] + 2, n_slices)
            def ya(j):
                hy = hy_t[j % 2]
                src = until_made(dve, ("hmT", j))
                until_taken(dve, ("zm", j))
                if j >= 2:
                    dve.wait_ge(sem("ya_lo_made"), j - 1)
                took(V.tensor_scalar(hy[:, :], src[:, :], vcol("a_head_norm_g", j), None, ALU.mult), ("hmT", j))
                until_taken(dve, ("hmT", j))
                dve.wait_ge(sem("xc_again"), j + 1)
                step(V.scalar_tensor_tensor(out=hy[:, :], in0=hx_t[j % 2][:, :], scalar=vcol("a_skip", j), in1=hy[:, :],
                                            op0=ALU.mult, op1=ALU.add))
                V.tensor_tensor(hy[:, :], hy[:, :], zmT[:, j, :], ALU.mult).then_inc(sem("ya_made"), 1)

            def ya_low(j):
                his[0] += 1
                dve.wait_ge(hi_made, his[0])
                dve.wait_ge(sem("ya_made"), j + 1)
                V.tensor_tensor(ya_lo[:, j, :], hy_t[j % 2][:, :], ya_hi[:, j, :].bitcast(F32), ALU.subtract)\
                    .then_inc(sem("ya_lo_made"), 1)

            def means(j):
                until_taken(dve, ("xp", j))
                x_ = px_t[j % 2]
                cur = x_
                for lev in range(j // 2 + 1):
                    back, nxt = 2 ** lev, ps_t[lev % 2]
                    V.tensor_copy(nxt[:, 0:back], cur[:, 0:back])
                    step(V.tensor_tensor(nxt[:, back:], cur[:, back:], cur[:, 0:SEQ - back], ALU.add))
                    cur = nxt
                w = 2 ** (j // 2 + 1)
                pm = pm_t[j % 2]
                step(V.scalar_tensor_tensor(out=pm[:, w:], in0=cur[:, w:], scalar=1.0 / w, in1=x_[:, w:], op0=ALU.mult, op1=ALU.subtract))
                step(V.tensor_tensor(pm[:, 0:w], cur[:, 0:w], const[:, C_RCNT + 16 * (j // 2):C_RCNT + 16 * (j // 2) + w], ALU.mult))
                step(V.tensor_tensor(pm[:, 0:w], pm[:, 0:w], x_[:, 0:w], ALU.subtract))
                split_sum(pm[:, :], poolT_hi[:, j, :], poolT_lo[:, j, :]).then_inc(sem("mean_made"), 1)

            for j in range(KC):
                ya(j)
                if j >= 1:
                    ya_low(j - 1)
                if j == 3:
                    until_made(dve, ("xp", 1))
                    split(slice_no[("xp", 0)] + 2, n_slices)
            ya_low(KC - 1)
            until_made(dve, ("xp", 3))
            split(slice_no[("xp", 1)] + 2, n_slices)
            for s in range(4):
                means(2 * s)
                means(2 * s + 1)
                name, k = (("xp", 2), ("xp", 3), ("zp", 0), ("zp", 1))[s]
                until_made(dve, (name, 2 * k + 1))
                split(slice_no[(name, k)] + 2, n_slices)
            for k in (2, 3):
                until_made(dve, ("zp", 2 * k + 1))
                split(slice_no[("zp", k)] + 2, n_slices)
            for j in range(KC):
                yb = yb_t[j % 2]
                src = until_made(dve, ("pool", j))
                until_taken(dve, ("zp", j))
                if j == 0:
                    dve.wait_ge(sem("ya_lo_made"), KC)
                step(V.scalar_tensor_tensor(out=yb[:, :], in0=src[:, :], scalar=vcol("a_pool_scale", j), in1=zpT[:, j, :],
                                            op0=ALU.mult, op1=ALU.mult))
                took(split_sum(yb[:, :], yb_hi[:, j, :], yb_lo[:, j, :]), ("pool", j))
            split(slice_no[("pool", 0)] + 2, n_slices)
            dve.wait_ge(sem("x3_back"), 16)
            for c in range(4):
                split(slice_no[("w_out2", c, 0)] + 2, n_slices)
                dve.wait_ge(sem("half_used"), c + 1)
                split(slice_no[("w_out2", c, 0)] + 3, n_slices)
                for tt in range(TT):
                    src = until_made(dve, ("w_out2", c, tt))
                    xv = x4_tok[:, tt, 256 * c:256 * c + 256]
                    took(V.tensor_tensor(xv, src[:, 0:256], xv, ALU.add), ("w_out2", c, tt))
            rsqrt(TT, D, 4 * TT, quarters=True)
            diagonals()
            for j in range(KC):
                evict_lo(("hT", 2, j), hT_hi[2][:, j, :], hT_lo[2][:, j, :], vcol("c_norm_g", j))
            step(V.tensor_copy(pos_f[:, :], pos_i[:, :]))
            step(V.tensor_tensor(ang[:, :, :], pos_f[:, :].unsqueeze(2).to_broadcast([P, TT, HALF]),
                                 const[:, C_INVF:C_INVF + HALF].unsqueeze(1).to_broadcast([P, TT, HALF]), ALU.mult))
            step(V.tensor_scalar(ang_k[:, :, :], ang[:, :, :], 1.0 / (2 * np.pi), None, ALU.mult))
            step(V.tensor_scalar(ang_k[:, :, :], ang_k[:, :, :], ROUNDER, None, ALU.add))
            step(V.tensor_scalar(ang_k[:, :, :], ang_k[:, :, :], -ROUNDER, None, ALU.add))
            for part in TWO_PI:
                step(V.scalar_tensor_tensor(out=ang[:, :, :], in0=ang_k[:, :, :], scalar=-part, in1=ang[:, :, :],
                                            op0=ALU.mult, op1=ALU.add))
            pi = 3.1415925
            V.tensor_scalar(ang[:, :, :], ang[:, :, :], pi, -pi, ALU.min, ALU.max).then_inc(sem("angle_made"), 1)
            dve.wait_ge(sem("angle_made"), 1)
            step(V.scalar_tensor_tensor(out=ang_k[:, :, :], in0=ang[:, :, :], scalar=-1.0, in1=ang[:, :, :], op0=ALU.mult, op1=ALU.max))
            V.tensor_scalar(ang_k[:, :, :], ang_k[:, :, :], -1.0, float(np.pi / 2), ALU.mult, ALU.add).then_inc(sem("angle_made"), 1)
            for s in range(3):
                until_made(dve, ("cin", s, 1))
                split(slice_no[("cin", s)] + 2, n_slices)
            rsqrt(2 * TT, ((0, TT, QL), (TT, 2 * TT, KVL)), 3 * TT)
            V.tensor_copy(kpes[:, 0:TT], ssq[:, 2 * TT:3 * TT])
            for tt in range(TT):
                V.tensor_scalar(c_tok[:, tt, 0:QL], c_tok[:, tt, 0:QL], rstd[:, tt:tt + 1], None, ALU.mult).then_inc(sem("c_normed"), 1)
                V.tensor_scalar(c_tok[:, tt, QL:QL + KVL], c_tok[:, tt, QL:QL + KVL], rstd[:, TT + tt:TT + tt + 1], None, ALU.mult)\
                    .then_inc(sem("c_normed"), 1)
            dve.wait_ge(sem("sines"), 2)
            dve.wait_ge(sem("gr_loaded"), 32)
            bc = lambda a: a.unsqueeze(1).to_broadcast([P, TT, HALF])
            both = lambda a: a.unsqueeze(2).to_broadcast([P, TT, 2, HALF])

            def rope_tables(k):
                for n, (c, half) in enumerate(((0, 0), (1, 1), (0, 1), (1, 0))):
                    ins = V.tensor_tensor(qtab[:, n, :, :], cs_t[:, c, :, :], bc(gr[:, k, half * HALF:(half + 1) * HALF]), ALU.mult)
                step(ins)

            rope_tables(1)
            k1_, k2_ = c_tok[:, :, QL + KVL:QL + KVL + HALF], c_tok[:, :, QL + KVL + HALF:]
            ra, rb = rp_a[:, 0:TT, :], rp_b[:, 0:TT, :]
            for dst, (a, ta, b, tb, op) in ((kpe[:, :, 0:HALF], (k1_, 0, k2_, 1, ALU.subtract)),
                                            (kpe[:, :, HALF:], (k2_, 2, k1_, 3, ALU.add))):
                V.tensor_tensor(ra, a, qtab[:, ta, :, :], ALU.mult)
                step(V.tensor_tensor(rb, b, qtab[:, tb, :, :], ALU.mult))
                step(V.tensor_tensor(dst, ra, rb, op))
            rope_tables(0)
            for s in range(4):
                until_made(dve, ("z3", 2 * s + 1))
                split(slice_no[("z3", s)] + 2, n_slices)
            for j in range(5):
                evict_lo(("cT", j), cT_hi[:, j, :], cT_lo[:, j, :], vec[:, V_QN + j:V_QN + j + 1])
            for s in range(4):
                split(slice_no[("uq", s)] + 2, n_slices)
                dve.wait_ge(sem("sq_made"), 2 * s + 1)
                V.tensor_reduce(ssq[:, 0:8].rearrange("p (t h) -> p t h", h=2), sq_t[0][:, :, :, :], AX_X, ALU.add)\
                    .then_inc(sem("sq_used"), 1)
                if s >= 1:
                    until_taken(dve, ("qpT", s - 1))
                q_a, q_b = qb[:, :, :, NOPE:NOPE + HALF], qb[:, :, :, NOPE + HALF:]
                ra4 = rp_a[:, :, :].rearrange("p (t h) n -> p t h n", h=2)
                rb4 = rp_b[:, :, :].rearrange("p (t h) n -> p t h n", h=2)
                for a, ta, b, tb, op, dst in ((q_a, 0, q_b, 1, ALU.subtract, qr[:, :, :, 0:HALF]),
                                              (q_b, 2, q_a, 3, ALU.add, qr[:, :, :, HALF:])):
                    V.tensor_tensor(ra4, a, both(qtab[:, ta, :, :]), ALU.mult)
                    step(V.tensor_tensor(rb4, b, both(qtab[:, tb, :, :]), ALU.mult))
                    if dst.shape == qr[:, :, :, HALF:].shape and op == ALU.add:
                        V.tensor_tensor(dst, ra4, rb4, op).then_inc(sem("q_roped"), 1)
                        dve.wait_ge(sem("q_roped"), s + 1)
                    else:
                        step(V.tensor_tensor(dst, ra4, rb4, op))
                split(slice_no[("ukv", s)] + 2, n_slices)
                dve.wait_ge(sem("sq_made"), 2 * s + 2)
                V.tensor_reduce(ssq[:, 8:16].rearrange("p (t h) -> p t h", h=2), sq_t[0][:, :, :, 0:NOPE], AX_X, ALU.add)\
                    .then_inc(sem("sq_used"), 1)
                dve.wait_ge(sem("sq_used"), 2 * s + 2)
                k_ssq = ssq[:, 8:16].rearrange("p (t h) -> p t h", h=2)
                step(V.tensor_tensor(k_ssq, k_ssq, kpes[:, 0:TT].unsqueeze(2).to_broadcast([P, TT, 2]), ALU.add))
                rsqrt(16, QKH, 0)
                rs = rstd[:, :].rearrange("p (k t h) -> p k t h", k=2, h=2)
                V.tensor_scalar(rq[:, :, 2 * s:2 * s + 2], rs[:, 0, :, :], C_SCALE, None, ALU.mult)
                if s >= 1:
                    until_taken(dve, ("kpT", s - 1))
                for h in range(2):
                    V.tensor_tensor(kb[:, :, h, :], kb[:, :, h, :], rs[:, 1, :, h:h + 1].to_broadcast([P, TT, NOPE]), ALU.mult)
                step(V.tensor_tensor(kr[:, :, 0, :], kpe[:, :, :], rs[:, 1, :, 0:1].to_broadcast([P, TT, ROPE]), ALU.mult))
                V.tensor_tensor(kr[:, :, 1, :], kpe[:, :, :], rs[:, 1, :, 1:2].to_broadcast([P, TT, ROPE]), ALU.mult)\
                    .then_inc(sem("k_normed"), 1)
            dve.wait_ge(sem("k_normed"), 4)

            def max3(i, src):
                step(V.tensor_reduce(neg_max[:, i % 8:i % 8 + 1], src, AX_X, ALU.max, negate=True))
                V.tensor_tensor(nb3[:, i % 8:i % 8 + 1], neg_max[:, i % 8:i % 8 + 1], rq[:, i % TT, i // TT:i // TT + 1], ALU.mult)\
                    .then_inc(sem("max3_made"), 1)

            attention(CH * TT, "S3", "PT3", "O3", max3, pT3_t, lambda k: o3_tok[:, k % TT, (k // TT) * VH:(k // TT + 1) * VH], VH)
            def y3_low(j):
                his[0] += 1
                dve.wait_ge(hi_made, his[0])
                until_taken(dve, ("OT3", j))
                V.tensor_tensor(yT3_lo[:, j, :], y3_t[j % 2][:, :], yT3_hi[:, j, :].bitcast(F32), ALU.subtract)\
                    .then_inc(sem("y3_lo_made"), 1)

            for j in range(KC):
                src = until_made(dve, ("OT3", j))
                until_taken(dve, ("z3", j))
                if j >= 2:
                    dve.wait_ge(sem("y3_lo_made"), j - 1)
                took(V.tensor_tensor(y3_t[j % 2][:, :], src[:, :], zT[:, j, :], ALU.mult), ("OT3", j))
                if j >= 1:
                    y3_low(j - 1)
            y3_low(KC - 1)
            for s in range(4):
                for tp in range(2):
                    src = until_made(dve, ("out3", s, tp))
                    xv = x4_tok[:, 2 * tp:2 * tp + 2, 256 * s:256 * s + 256]
                    took(V.tensor_tensor(xv, src[:, :].rearrange("p (t n) -> p t n", t=2), xv, ALU.add), ("out3", s, tp))
                split(slice_no[("out3", s)] + 2, n_slices)


def kernel(**inputs):
    import concourse.bacc as bacc
    from concourse.bass_utils import run_bass_kernel_spmd

    a = {k: np.asarray(v) for k, v in inputs.items()}
    cols = lambda v: np.ascontiguousarray(v.reshape(-1, P).T)
    pad = lambda v: np.concatenate([v, np.zeros(P - len(v), v.dtype)])[:, None]
    vec_of = {
        "norm_mix_g": a["norm_mix_g"], "conv_b": a["conv_b"], "norm_ffn_g": a["norm_ffn_g"], "a_norm_g": a["a_norm_g_2"][0],
        "a_conv_b": a["a_conv_b_2"][0], "a_head_norm_g": a["a_head_norm_g_2"][0], "a_skip": a["a_skip_2"][0],
        "a_pool_scale": a["a_pool_scale_2"][0], "c_norm_g": a["c_norm_g_2"][0],
        **{f"conv_w{i}": a["conv_w"][i] for i in range(3)},
        **{f"a_conv_w{i}": a["a_conv_w_2"][0, i] for i in range(4)},
    }
    router = np.concatenate([a["w_router_group"], a["w_router_expert"].transpose(1, 0, 2).reshape(D, NE)], axis=1)
    w_forget, w_gates = np.zeros((D, P), np.float32), np.zeros((D, P), np.float32)
    w_forget[:, 0:H1] = a["w_in"][:, 6 * D:6 * D + H1]
    w_gates[:, 0:MH] = a["a_w_in_2"][0][:, 2 * D:2 * D + MH]
    w_gates[:, LO:LO + MH] = a["a_w_in_2"][0][:, 2 * D + MH:2 * D + 2 * MH]
    chunks = lambda w: w.reshape(KC, P, -1).transpose(1, 0, 2)
    arrays = {
        "x": a["x"][0],
        "w_forget": chunks(w_forget),
        "w_gates": chunks(w_gates),
        "consts": constants(),
        "vecs": np.concatenate([cols(vec_of[n]) for n in VECS] + [
            cols(a["c_q_norm_g_2"][0]), cols(a["c_kv_norm_g_2"][0]), cols(a["c_qn_g_2"][0, :NOPE]), cols(a["c_kn_g_2"][0, :NOPE]),
            pad(a["b_forget"]), pad(a["a_b_if_2"][0, :MH]), pad(a["a_b_if_2"][0, MH:])], axis=1),
        "positions": np.ascontiguousarray(a["positions_2"][0].reshape(TT, P).T),
        "w_router": chunks(router),
        "norm_final_g": a["norm_final_g"],
        "c_qn_rope_g": a["c_qn_g_2"][0, NOPE:],
        "c_kn_rope_g": a["c_kn_g_2"][0, NOPE:],
        "w_in": a["w_in"], "w_conv_out": a["w_conv_out"], "w_att_out": a["w_att_out"], "w_out": a["w_out"],
        "w_e_gate": a["w_e_gate"], "w_e_up": a["w_e_up"], "w_e_down": a["w_e_down"],
        "a_w_in": a["a_w_in_2"][0], "a_w_q": a["a_w_q_2"][0], "a_w_k": a["a_w_k_2"][0], "a_w_v": a["a_w_v_2"][0],
        "a_pool_w": a["a_pool_w_2"][0], "a_w_out": a["a_w_out_2"][0], "c_w_in": a["c_w_in_2"][0], "c_w_uq": a["c_w_uq_2"][0],
        "c_w_ukv": a["c_w_ukv_2"][0], "c_w_out": a["c_w_out_2"][0],
    }
    arrays = {k: np.ascontiguousarray(v) for k, v in arrays.items()}
    nc = bacc.Bacc("TRN2", target_bir_lowering=False, num_devices=1)
    t = {k: nc.dram_tensor(f"in_{k}", v.shape, mybir.dt.from_np(v.dtype), kind="ExternalInput").ap() for k, v in arrays.items()}
    t["out"] = nc.dram_tensor("out_x", (SEQ, D), F32, kind="ExternalOutput").ap()
    build_kernel(nc, t)
    r = run_bass_kernel_spmd(nc, [{f"in_{k}": v for k, v in arrays.items()}], core_ids=[0])
    return r.results[0]["out_x"].reshape(1, SEQ, D)
```
